# Optimizing a Trainium2 kernel written in Bass

```python
import math
import jax
import jax.numpy as jnp
from jax import lax
import numpy as np

D_MODEL = 1024
BATCH = 1
SEQ = 256
DEPTH = 1

MIX_WIDTH = D_MODEL
PLE_DIM = 256
DA_WIDTH = MIX_WIDTH // 2
DA_HEADS = 4
DA_V_DIM = DA_WIDTH // DA_HEADS
DA_HEAD_DIM = DA_V_DIM // 2
ROT_DIM = DA_HEAD_DIM // 4
ROPE_THETA = 500000.0
Q_BLOCK = 128
HG_WIDTH = MIX_WIDTH - DA_WIDTH
HG_HEADS = 4
HG_KEY_DIM = HG_WIDTH // HG_HEADS
HG_VAL_DIM = HG_WIDTH // HG_HEADS
CHUNK = 64
D_FF = 2816
CONV_WIDTH = 3
EPS = 1e-6

IN_SPLIT_SIZES = (
    DA_HEADS * 2 * DA_HEAD_DIM,
    DA_HEADS * 2 * DA_HEAD_DIM,
    DA_HEADS * DA_V_DIM,
    HG_HEADS * HG_KEY_DIM,
    HG_HEADS * HG_KEY_DIM,
    HG_HEADS * HG_KEY_DIM,
    HG_HEADS * HG_VAL_DIM,
    HG_HEADS * HG_VAL_DIM,
)
IN_COLS = sum(IN_SPLIT_SIZES)
IN_SPLIT_POINTS = tuple(int(c) for c in np.cumsum(IN_SPLIT_SIZES)[:-1])


def rmsnorm(x, g, eps=EPS):
    xf = x.astype(jnp.float32)
    y = xf * lax.rsqrt(jnp.mean(xf * xf, axis=-1, keepdims=True) + eps)
    return (y * g.astype(jnp.float32)).astype(x.dtype)

def partial_rotary(t, positions):
    half = ROT_DIM // 2
    inv_freq = ROPE_THETA ** (-jnp.arange(half, dtype=jnp.float32) / half)
    ang = positions.astype(jnp.float32)[..., None] * inv_freq
    cos = jnp.cos(ang)[:, :, None, None, :]
    sin = jnp.sin(ang)[:, :, None, None, :]
    tr = t[..., :ROT_DIM].astype(jnp.float32)
    x1, x2 = tr[..., :half], tr[..., half:]
    rot = jnp.concatenate([x1 * cos - x2 * sin, x2 * cos + x1 * sin], axis=-1)
    return jnp.concatenate([rot.astype(t.dtype), t[..., ROT_DIM:]], axis=-1)

def diff_attention(q, k, v, lam_q1, lam_k1, lam_q2, lam_k2, subln_g, lambda_init):
    B, S = q.shape[0], q.shape[1]
    f32 = jnp.float32
    lam = (jnp.exp(jnp.sum(lam_q1.astype(f32) * lam_k1.astype(f32)))
           - jnp.exp(jnp.sum(lam_q2.astype(f32) * lam_k2.astype(f32))) + lambda_init)
    scale = DA_HEAD_DIM ** -0.5
    qb = (q * scale).reshape(B, S // Q_BLOCK, Q_BLOCK, DA_HEADS, 2, DA_HEAD_DIM)
    qb = qb.transpose(1, 0, 2, 3, 4, 5)

    def block(qblk):
        s = jnp.einsum('bqhmd,bkhmd->bhmqk', qblk, k, preferred_element_type=f32)
        a = jax.nn.softmax(s, axis=-1)
        w = a[:, :, 0] - lam * a[:, :, 1]
        return jnp.einsum('bhqk,bkhe->bqhe', w.astype(v.dtype), v)

    o = lax.map(block, qb)
    o = o.transpose(1, 0, 2, 3, 4).reshape(B, S, DA_HEADS, DA_V_DIM)
    o = rmsnorm(o, subln_g) * (1.0 - lambda_init)
    return o.reshape(B, S, DA_HEADS * DA_V_DIM)

def _to_chunks(t):
    z, b, s, h, e = t.shape
    return t.reshape(z, b, s // CHUNK, CHUNK, h, e).transpose(2, 0, 1, 4, 3, 5)

def hgrn2_bidirectional(q, zf, zb, v, g, lb_gamma, norm_g, layer):
    B, S = q.shape[0], q.shape[1]
    f32 = jnp.float32
    H, dk, dv = HG_HEADS, HG_KEY_DIM, HG_VAL_DIM
    lb_all = jnp.cumsum(jax.nn.softmax(lb_gamma.astype(f32), axis=1), axis=1)
    lb = lb_all[:, layer].reshape(2, 1, 1, H, dk)
    q4 = q.reshape(B, S, H, dk).astype(f32)
    v4 = v.reshape(B, S, H, dv).astype(f32)
    z = jnp.stack([zf.reshape(B, S, H, dk), zb.reshape(B, S, H, dk)[:, ::-1]], 0).astype(f32)
    log_f = jnp.log(lb + (1.0 - lb) * jax.nn.sigmoid(z))
    k_in = (1.0 - lb) * jax.nn.sigmoid(-z)
    qd = jnp.stack([q4, q4[:, ::-1]], 0)
    vd = jnp.stack([v4, v4[:, ::-1]], 0)
    xs = (_to_chunks(qd), _to_chunks(k_in), _to_chunks(vd), _to_chunks(log_f))
    tri = jnp.tril(jnp.ones((CHUNK, CHUNK), dtype=bool))[:, :, None]

    def step(state, inp):
        qc, kc, vc, gc = inp
        bcum = jnp.cumsum(gc, axis=-2)
        b_last = bcum[..., -1:, :]
        o_inter = jnp.einsum('zbhtk,zbhkv->zbhtv', qc * jnp.exp(bcum), state)
        diff = bcum[..., :, None, :] - bcum[..., None, :, :]
        decay = jnp.exp(jnp.where(tri, diff, -jnp.inf))
        attn = jnp.einsum('zbhtk,zbhtsk->zbhts', qc, decay * kc[..., None, :, :])
        o_intra = jnp.einsum('zbhts,zbhsv->zbhtv', attn, vc)
        k_dec = kc * jnp.exp(b_last - bcum)
        new_state = (jnp.exp(b_last[..., 0, :])[..., None] * state
                     + jnp.einsum('zbhsk,zbhsv->zbhkv', k_dec, vc))
        return new_state, o_inter + o_intra

    state0 = jnp.zeros((2, B, H, dk, dv), f32)
    _, ys = lax.scan(step, state0, xs)
    ys = ys.transpose(1, 2, 0, 4, 3, 5).reshape(2, B, S, H, dv)
    o = ys[0] + ys[1][:, ::-1]
    o = rmsnorm(o, norm_g) * jax.nn.silu(g.reshape(B, S, H, dv).astype(f32))
    return o.reshape(B, S, H * dv).astype(q.dtype)

def conv_glu(h, w_gate, w_up, conv_w, conv_b, w_down):
    S = h.shape[1]
    a = h @ w_gate
    u = h @ w_up
    pad = CONV_WIDTH // 2
    ap = jnp.pad(a, ((0, 0), (pad, pad), (0, 0)))
    c = conv_b
    for j in range(CONV_WIDTH):
        c = c + ap[:, j:j + S] * conv_w[j]
    return (jax.nn.gelu(c, approximate=False) * u) @ w_down

def first_inputs(seed: int = 0) -> dict:
    key = jax.random.key(seed)
    ks = jax.random.split(key, 24)
    f32 = jnp.float32

    def nrm(k, shape, scale):
        return jax.random.normal(k, shape, f32) * scale

    def gain(k, shape):
        return 1.0 + 0.05 * jax.random.normal(k, shape, f32)

    x = nrm(ks[0], (BATCH, SEQ, D_MODEL), 1.0)
    p = nrm(ks[1], (DEPTH, BATCH, SEQ, PLE_DIM), 1.0)
    offsets = jax.random.randint(ks[2], (BATCH, 1), 0, 1024, dtype=jnp.int32)
    positions = offsets + jnp.arange(SEQ, dtype=jnp.int32)[None, :]
    return {
        "x": x,
        "p": p,
        "positions": positions,
        "norm_mix_g": gain(ks[3], (DEPTH, D_MODEL)),
        "w_in": nrm(ks[4], (DEPTH, D_MODEL, IN_COLS), D_MODEL ** -0.5),
        "lam_q1": nrm(ks[5], (DEPTH, DA_HEAD_DIM), 0.1),
        "lam_k1": nrm(ks[6], (DEPTH, DA_HEAD_DIM), 0.1),
        "lam_q2": nrm(ks[7], (DEPTH, DA_HEAD_DIM), 0.1),
        "lam_k2": nrm(ks[8], (DEPTH, DA_HEAD_DIM), 0.1),
        "da_subln_g": gain(ks[9], (DEPTH, DA_V_DIM)),
        "hg_lb_gamma": gain(ks[10], (2, DEPTH + 1, HG_HEADS * HG_KEY_DIM)),
        "hg_norm_g": gain(ks[11], (DEPTH, HG_VAL_DIM)),
        "w_out": nrm(ks[12], (DEPTH, MIX_WIDTH, D_MODEL), MIX_WIDTH ** -0.5),
        "norm_ffn_g": gain(ks[13], (DEPTH, D_MODEL)),
        "w_ffn_gate": nrm(ks[14], (DEPTH, D_MODEL, D_FF), D_MODEL ** -0.5),
        "w_ffn_up": nrm(ks[15], (DEPTH, D_MODEL, D_FF), D_MODEL ** -0.5),
        "ffn_conv_w": nrm(ks[16], (DEPTH, CONV_WIDTH, D_FF), CONV_WIDTH ** -0.5),
        "ffn_conv_b": nrm(ks[17], (DEPTH, D_FF), 0.02),
        "w_ffn_down": nrm(ks[18], (DEPTH, D_FF, D_MODEL), D_FF ** -0.5),
        "norm_ple_g": gain(ks[19], (DEPTH, D_MODEL)),
        "w_ple": nrm(ks[20], (DEPTH, PLE_DIM, D_MODEL), PLE_DIM ** -0.5),
        "w_ple_gate": nrm(ks[21], (DEPTH, D_MODEL, D_MODEL), D_MODEL ** -0.5),
        "final_norm_g": gain(ks[22], (D_MODEL,)),
    }

def first_block(x, p, positions, norm_mix_g, w_in, lam_q1, lam_k1, lam_q2, lam_k2,
              da_subln_g, hg_lb_gamma, hg_norm_g, w_out, norm_ffn_g, w_ffn_gate,
              w_ffn_up, ffn_conv_w, ffn_conv_b, w_ffn_down, norm_ple_g, w_ple,
              w_ple_gate, final_norm_g):
    B, S = x.shape[0], x.shape[1]
    for i in range(DEPTH):
        h = rmsnorm(x, norm_mix_g[i])
        proj = h @ w_in[i]
        da_q, da_k, da_v, hg_q, hg_zf, hg_zb, hg_v, hg_g = jnp.split(proj, IN_SPLIT_POINTS, axis=-1)
        da_q = partial_rotary(da_q.reshape(B, S, DA_HEADS, 2, DA_HEAD_DIM), positions)
        da_k = partial_rotary(da_k.reshape(B, S, DA_HEADS, 2, DA_HEAD_DIM), positions)
        da_v = da_v.reshape(B, S, DA_HEADS, DA_V_DIM)
        lambda_init = 0.8 - 0.6 * math.exp(-0.3 * i)
        o_da = diff_attention(da_q, da_k, da_v, lam_q1[i], lam_k1[i], lam_q2[i], lam_k2[i],
                              da_subln_g[i], lambda_init)
        o_hg = hgrn2_bidirectional(hg_q, hg_zf, hg_zb, hg_v, hg_g, hg_lb_gamma, hg_norm_g[i], i)
        x = x + jnp.concatenate([o_da, o_hg], axis=-1) @ w_out[i]
        x = x + conv_glu(rmsnorm(x, norm_ffn_g[i]), w_ffn_gate[i], w_ffn_up[i],
                         ffn_conv_w[i], ffn_conv_b[i], w_ffn_down[i])
        gate = jax.nn.sigmoid(rmsnorm(x, norm_ple_g[i]) @ w_ple_gate[i])
        x = x + (p[i] @ w_ple[i]) * gate
    return rmsnorm(x, final_norm_g)


HEAD_DIM = 64
FOX_HEADS = 8
DSA_HEADS = 8
IDX_HEADS = 8
IDX_DIM = 32
TOPK_MAX = 256
ROPE_FRACTION = 4
N_SUBLAYERS = 3
NORM_EPS = 1e-6
FOX_WIDTH = FOX_HEADS * HEAD_DIM
DSA_WIDTH = DSA_HEADS * HEAD_DIM
IN_SIZES = (FOX_WIDTH, FOX_WIDTH, FOX_WIDTH, FOX_HEADS, DSA_WIDTH, HEAD_DIM, HEAD_DIM, IDX_HEADS * IDX_DIM, IDX_DIM, IDX_HEADS, D_MODEL, D_MODEL)
D_IN = sum(IN_SIZES)


def rms_norm(x, g):
    xf = x.astype(jnp.float32)
    y = xf * lax.rsqrt(jnp.mean(xf * xf, axis=-1, keepdims=True) + NORM_EPS)
    return (y * g.astype(jnp.float32)).astype(x.dtype)

def modulate(x, g, shift, scale):
    return rms_norm(x, g) * (1 + scale[:, None, :]) + shift[:, None, :]

def swiglu(h, w1, w3, w2):
    return (jax.nn.silu(h @ w1) * (h @ w3)) @ w2

def rope_tables(positions, rot_dim):
    inv_freq = ROPE_THETA ** (-jnp.arange(0, rot_dim, 2, dtype=jnp.float32) / rot_dim)
    ang = positions.astype(jnp.float32)[..., None] * inv_freq
    return jnp.cos(ang), jnp.sin(ang)

def partial_rope(x, cos, sin):
    half = cos.shape[-1]
    x1 = x[..., :half].astype(jnp.float32)
    x2 = x[..., half:2 * half].astype(jnp.float32)
    r1 = (x1 * cos - x2 * sin).astype(x.dtype)
    r2 = (x2 * cos + x1 * sin).astype(x.dtype)
    return jnp.concatenate([r1, r2, x[..., 2 * half:]], axis=-1)

def fox_attention(q, k, v, log_f):
    B, S, H, dh = q.shape
    F = jnp.cumsum(log_f.astype(jnp.float32), axis=1).transpose(0, 2, 1)
    kpos = jnp.arange(S)
    scale = dh ** -0.5

    def block(i):
        qs = i * Q_BLOCK
        qb = lax.dynamic_slice_in_dim(q, qs, Q_BLOCK, axis=1)
        Fq = lax.dynamic_slice_in_dim(F, qs, Q_BLOCK, axis=2)
        s = jnp.einsum('bqhd,bkhd->bhqk', qb, k, preferred_element_type=jnp.float32) * scale
        s = s + Fq[..., None] - F[:, :, None, :]
        qpos = qs + jnp.arange(Q_BLOCK)
        mask = kpos[None, :] <= qpos[:, None]
        s = jnp.where(mask[None, None], s, -jnp.inf)
        p = jax.nn.softmax(s, axis=-1)
        return jnp.einsum('bhqk,bkhd->bqhd', p.astype(v.dtype), v)

    out = lax.map(block, jnp.arange(S // Q_BLOCK))
    return out.transpose(1, 0, 2, 3, 4).reshape(B, S, H, dh)

def dsa_attention(q, k, v, iq, ik, iw, top_k):
    B, S, H, dh = q.shape
    kchunk = jnp.arange(S) // CHUNK
    scale = dh ** -0.5
    idx_scale = IDX_DIM ** -0.5

    def block(i):
        qs = i * Q_BLOCK
        qb = lax.dynamic_slice_in_dim(q, qs, Q_BLOCK, axis=1)
        iqb = lax.dynamic_slice_in_dim(iq, qs, Q_BLOCK, axis=1)
        iwb = lax.dynamic_slice_in_dim(iw, qs, Q_BLOCK, axis=1)
        qchunk = (qs + jnp.arange(Q_BLOCK)) // CHUNK
        admissible = kchunk[None, :] <= qchunk[:, None]
        dots = jnp.einsum('bqhd,bkd->bqhk', iqb, ik, preferred_element_type=jnp.float32) * idx_scale
        score = jnp.einsum('bqh,bqhk->bqk', iwb.astype(jnp.float32), jax.nn.relu(dots))
        score = jnp.where(admissible[None], score, -jnp.inf)
        _, sel = lax.top_k(score, top_k)
        kg = jax.vmap(lambda kb, ib: kb[ib])(k, sel)
        vg = jax.vmap(lambda vb, ib: vb[ib])(v, sel)
        valid = (sel // CHUNK) <= qchunk[None, :, None]
        s = jnp.einsum('bqhd,bqkd->bhqk', qb, kg, preferred_element_type=jnp.float32) * scale
        s = jnp.where(valid[:, None], s, -jnp.inf)
        p = jax.nn.softmax(s, axis=-1)
        return jnp.einsum('bhqk,bqkd->bqhd', p.astype(vg.dtype), vg)

    out = lax.map(block, jnp.arange(S // Q_BLOCK))
    return out.transpose(1, 0, 2, 3, 4).reshape(B, S, H, dh)

def hybrid_mixer(h, w_in, fox_f_bias, fox_qk_g, dsa_qk_g, w_br_fox, w_br_dsa, w_out, rope_a, rope_i, top_k):
    B, S, _ = h.shape
    cos_a, sin_a = rope_a
    cos_i, sin_i = rope_i
    z = h @ w_in
    split_points = [int(p) for p in np.cumsum(IN_SIZES)[:-1]]
    (fq, fk, fv, ff, dq, dk, dv, iq, ik, iw, ga, gb) = jnp.split(z, split_points, axis=-1)
    fq = rms_norm(fq.reshape(B, S, FOX_HEADS, HEAD_DIM), fox_qk_g[0])
    fk = rms_norm(fk.reshape(B, S, FOX_HEADS, HEAD_DIM), fox_qk_g[1])
    fv = fv.reshape(B, S, FOX_HEADS, HEAD_DIM)
    log_f = jax.nn.log_sigmoid(ff.astype(jnp.float32) + fox_f_bias.astype(jnp.float32))
    ya = fox_attention(fq, fk, fv, log_f).reshape(B, S, FOX_WIDTH)
    dq = partial_rope(rms_norm(dq.reshape(B, S, DSA_HEADS, HEAD_DIM), dsa_qk_g[0]), cos_a[:, :, None, :], sin_a[:, :, None, :])
    dk = partial_rope(rms_norm(dk, dsa_qk_g[1]), cos_a, sin_a)
    iq = partial_rope(iq.reshape(B, S, IDX_HEADS, IDX_DIM), cos_i[:, :, None, :], sin_i[:, :, None, :])
    ik = partial_rope(ik, cos_i, sin_i)
    iw = iw * (IDX_HEADS ** -0.5)
    yb = dsa_attention(dq, dk, dv, iq, ik, iw, top_k).reshape(B, S, DSA_WIDTH)
    merged = jax.nn.sigmoid(ga) * (ya @ w_br_fox) + jax.nn.sigmoid(gb) * (yb @ w_br_dsa)
    return merged @ w_out

def second_inputs(seed: int = 0) -> dict:
    key = jax.random.key(seed)
    ks = jax.random.split(key, 24)
    L = DEPTH

    def nrm(k, shape, fan_in, gain=1.0):
        return jax.random.normal(k, shape, jnp.float32) * (gain * fan_in ** -0.5)

    x = jax.random.normal(ks[0], (BATCH, SEQ, D_MODEL), jnp.float32)
    c = jax.random.normal(ks[1], (BATCH, D_MODEL), jnp.float32)
    offsets = jax.random.randint(ks[2], (BATCH, 1), 0, 1024) * CHUNK
    positions = (offsets + jnp.arange(SEQ, dtype=jnp.int32)[None, :]).astype(jnp.int32)
    ada_w = nrm(ks[3], (L, D_MODEL, 3 * N_SUBLAYERS * D_MODEL), D_MODEL, 0.5)
    ada_b = 0.02 * jax.random.normal(ks[4], (L, 3 * N_SUBLAYERS * D_MODEL), jnp.float32)
    norm_g = 1.0 + 0.05 * jax.random.normal(ks[5], (L, N_SUBLAYERS, D_MODEL), jnp.float32)
    ffn1_w1 = nrm(ks[6], (L, D_MODEL, D_FF), D_MODEL)
    ffn1_w3 = nrm(ks[7], (L, D_MODEL, D_FF), D_MODEL)
    ffn1_w2 = nrm(ks[8], (L, D_FF, D_MODEL), D_FF)
    w_in = nrm(ks[9], (L, D_MODEL, D_IN), D_MODEL)
    fox_f_bias = 2.0 + 0.1 * jax.random.normal(ks[10], (L, FOX_HEADS), jnp.float32)
    fox_qk_g = 1.0 + 0.05 * jax.random.normal(ks[11], (L, 2, HEAD_DIM), jnp.float32)
    dsa_qk_g = 1.0 + 0.05 * jax.random.normal(ks[12], (L, 2, HEAD_DIM), jnp.float32)
    w_br_fox = nrm(ks[13], (L, FOX_WIDTH, D_MODEL), FOX_WIDTH)
    w_br_dsa = nrm(ks[14], (L, DSA_WIDTH, D_MODEL), DSA_WIDTH)
    w_out = nrm(ks[15], (L, D_MODEL, D_MODEL), D_MODEL)
    ffn2_w1 = nrm(ks[16], (L, D_MODEL, D_FF), D_MODEL)
    ffn2_w3 = nrm(ks[17], (L, D_MODEL, D_FF), D_MODEL)
    ffn2_w2 = nrm(ks[18], (L, D_FF, D_MODEL), D_FF)
    return {'x': x, 'c': c, 'positions': positions, 'ada_w': ada_w, 'ada_b': ada_b,
            'norm_g': norm_g, 'ffn1_w1': ffn1_w1, 'ffn1_w3': ffn1_w3, 'ffn1_w2': ffn1_w2,
            'w_in': w_in, 'fox_f_bias': fox_f_bias, 'fox_qk_g': fox_qk_g, 'dsa_qk_g': dsa_qk_g,
            'w_br_fox': w_br_fox, 'w_br_dsa': w_br_dsa, 'w_out': w_out,
            'ffn2_w1': ffn2_w1, 'ffn2_w3': ffn2_w3, 'ffn2_w2': ffn2_w2}

def second_block(x, c, positions, ada_w, ada_b, norm_g, ffn1_w1, ffn1_w3, ffn1_w2, w_in, fox_f_bias, fox_qk_g, dsa_qk_g, w_br_fox, w_br_dsa, w_out, ffn2_w1, ffn2_w3, ffn2_w2):
    B, S, _ = x.shape
    top_k = min(TOPK_MAX, S // 4)
    rope_a = rope_tables(positions, HEAD_DIM // ROPE_FRACTION)
    rope_i = rope_tables(positions, IDX_DIM // ROPE_FRACTION)
    cond = jax.nn.silu(c)
    for l in range(DEPTH):
        mod = (cond @ ada_w[l] + ada_b[l]).reshape(B, N_SUBLAYERS, 3, D_MODEL)
        h = modulate(x, norm_g[l, 0], mod[:, 0, 0], mod[:, 0, 1])
        x = x + 0.5 * mod[:, 0, 2][:, None, :] * swiglu(h, ffn1_w1[l], ffn1_w3[l], ffn1_w2[l])
        h = modulate(x, norm_g[l, 1], mod[:, 1, 0], mod[:, 1, 1])
        y = hybrid_mixer(h, w_in[l], fox_f_bias[l], fox_qk_g[l], dsa_qk_g[l], w_br_fox[l], w_br_dsa[l], w_out[l], rope_a, rope_i, top_k)
        x = x + mod[:, 1, 2][:, None, :] * y
        h = modulate(x, norm_g[l, 2], mod[:, 2, 0], mod[:, 2, 1])
        x = x + 0.5 * mod[:, 2, 2][:, None, :] * swiglu(h, ffn2_w1[l], ffn2_w3[l], ffn2_w2[l])
    return x


def setup_inputs(seed=0):
    out = dict(first_inputs(seed))
    for name, value in second_inputs(seed + 1).items():
        if name != "x":
            out[name + "_2"] = value
    return out


def reference(
    x, p, positions, norm_mix_g, w_in, lam_q1, lam_k1, lam_q2, lam_k2, da_subln_g, hg_lb_gamma,
    hg_norm_g, w_out, norm_ffn_g, w_ffn_gate, w_ffn_up, ffn_conv_w, ffn_conv_b, w_ffn_down,
    norm_ple_g, w_ple, w_ple_gate, final_norm_g, c_2, positions_2, ada_w_2, ada_b_2, norm_g_2,
    ffn1_w1_2, ffn1_w3_2, ffn1_w2_2, w_in_2, fox_f_bias_2, fox_qk_g_2, dsa_qk_g_2, w_br_fox_2,
    w_br_dsa_2, w_out_2, ffn2_w1_2, ffn2_w3_2, ffn2_w2_2,
):
    x = first_block(
        x, p, positions, norm_mix_g, w_in, lam_q1, lam_k1, lam_q2, lam_k2, da_subln_g,
        hg_lb_gamma, hg_norm_g, w_out, norm_ffn_g, w_ffn_gate, w_ffn_up, ffn_conv_w, ffn_conv_b,
        w_ffn_down, norm_ple_g, w_ple, w_ple_gate, final_norm_g,
    )
    return second_block(
        x, c_2, positions_2, ada_w_2, ada_b_2, norm_g_2, ffn1_w1_2, ffn1_w3_2, ffn1_w2_2,
        w_in_2, fox_f_bias_2, fox_qk_g_2, dsa_qk_g_2, w_br_fox_2, w_br_dsa_2, w_out_2,
        ffn2_w1_2, ffn2_w3_2, ffn2_w2_2,
    )


_drawn_inputs = setup_inputs


def setup_inputs(seed=0):
    import zlib

    import numpy as np

    out = dict(_drawn_inputs(seed))
    spreads = {}
    factors = {'lam_q1': 8.0,
     'lam_k2': 2.871,
     'hg_lb_gamma': 3.599,
     'hg_norm_g': 2.838,
     'ffn_conv_b': 5.91,
     'norm_ple_g': 7.328,
     'ada_b_2': 3.561,
     'norm_g_2': 4.03,
     'fox_f_bias_2': 64.0,
     'fox_qk_g_2': 8.0,
     'dsa_qk_g_2': 8.0}
    for name, (base, spread) in spreads.items():
        noise = np.random.default_rng([zlib.crc32(name.encode()), seed]).standard_normal(out[name].shape)
        drawn = base * np.exp(spread * noise) if base else spread * noise
        out[name] = jnp.asarray(drawn.astype(out[name].dtype))
    for name, factor in factors.items():
        out[name] = (out[name] * factor).astype(out[name].dtype)
    return out
```

```python
from contextlib import ExitStack

import numpy as np

import concourse.bass as bass
from concourse import mybir

ALU = mybir.AluOpType
ACT = mybir.ActivationFunctionType
F32 = mybir.dt.float32
F32R = mybir.dt.float32r
I32 = mybir.dt.int32
AXX = mybir.AxisListType.X

P = 128
S = 256
TT = S // P
D = 1024
KT = D // P
FF = 2816
FSTEP = FF // 256
EPS = 1e-6
BIG = -1e30
PICKED = -3e38
TOPK = S // 4
LAMBDA_INIT = 0.2
THETA = 500000.0

IN1, OUT1, FFN1, PLE, PGATE = 0, 16, 20, 53, 54
FFN2, IN2, BRANCH, OUT2, FFN3, CHUNKS = 58, 91, 110, 114, 118, 151
RING = 3

IN1_COLS = [("zf", 2048), ("zf", 2304), ("zb", 2560), ("zb", 2816), ("g", 3584), ("g", 3840),
            ("hq", 1536), ("hq", 1792), ("hv", 3072), ("hv", 3328), ("dq", 0), ("dq", 256),
            ("dk", 512), ("dk", 768), ("dv", 1024), ("dv", 1280)]
IN2_COLS = [("fq", 0), ("fq", 256), ("fk", 512), ("fk", 768), ("dq", 1544), ("dq", 1800),
            ("misc", 0), ("misc", 1), ("iq", 2184), ("fv", 1024), ("fv", 1280),
            ("ga", 2480), ("ga", 2736), ("ga", 2992), ("ga", 3248),
            ("gb", 3504), ("gb", 3760), ("gb", 4016), ("gb", 4272)]
MISC = [[(0, 2056, 64), (64, 2056, 64)] + [(128 + 32 * i, 2440, 32) for i in range(4)],
        [(0, 2472, 8), (8, 1536, 8), (64, 2120, 64)]]

ROWS_A = [("conv_w", 66), ("conv_b", 22), ("norm_mix", 8), ("norm_ffn", 8), ("norm_ple", 8),
          ("final", 8), ("subln", 1), ("hgnorm", 1)]
ROWS_B = [("ada_b", 72), ("norm_g", 24), ("c", 8), ("gamma", 16), ("foxg", 2), ("dsag", 2)]


def offsets(rows):
    at, out = 0, {}
    for name, n in rows:
        out[name] = at
        at += n
    return out, at


COL_A, NROW_A = offsets(ROWS_A)
COL_B, NROW_B = offsets(ROWS_B)

LEVELS = [128, 64, 32, 16, 8, 4, 2]
CONST = [("ident", 128), ("rotA", 128), ("rotI", 128), ("mean64", 128), ("causal", 256),
         ("admit", 256), ("levels", 128 * (len(LEVELS) - 1)), ("freq", 2)]
CONST_AT, CONST_N = offsets(CONST)


def constants():
    out = np.zeros((P, CONST_N), np.float32)
    p = np.arange(P)

    def part(name):
        at = CONST_AT[name]
        return out[:, at:at + dict(CONST)[name]]

    part("ident")[p, p] = 1.0
    for name, period, half in (("rotA", 64, 8), ("rotI", 32, 4)):
        for m in range(P):
            if m % period < half:
                part(name)[m + half, m] = -1.0
            elif m % period < 2 * half:
                part(name)[m - half, m] = 1.0
    part("mean64")[:, :] = (p[:, None] // 64 == p[None, :] // 64) / 64.0
    part("causal")[:, P:] = np.where(p[None, :] <= p[:, None], 0.0, BIG)
    part("admit")[:, P:] = np.where(p[None, :] // 64 <= p[:, None] // 64, 0.0, BIG)
    for n, b in enumerate(LEVELS[1:]):
        same = p[:, None] // b == p[None, :] // b
        halves = p[:, None] // (b // 2) != p[None, :] // (b // 2)
        part("levels")[:, n * P:(n + 1) * P] = same & halves
    f_a = np.float32(THETA) ** (-np.arange(8, dtype=np.float32) / np.float32(8))
    f_i = np.float32(THETA) ** (-np.arange(0, 8, 2, dtype=np.float32) / np.float32(8))
    for m in range(P):
        if m % 64 < 16:
            part("freq")[m, 0] = f_a[m % 8]
        if m % 32 < 8:
            part("freq")[m, 1] = f_i[m % 4]
    return out


def two_blocks(nc, A, out):
    with ExitStack() as ctx:
        def sb(name, shape, dt=F32):
            return ctx.enter_context(nc.sbuf_tensor(name, [P] + shape, dt))

        def ps(name, shape):
            return ctx.enter_context(nc.psum_tensor(name, [P] + shape, F32))

        sems = {}

        def sem(name):
            if name not in sems:
                sems[name] = ctx.enter_context(nc.semaphore(name))
            return sems[name]

        raw = [sb(f"raw{r}", [2048]) for r in range(RING)]
        whi = [sb(f"whi{r}", [2048], F32R) for r in range(RING)]
        wlo = [sb(f"wlo{r}", [2048], F32R) for r in range(RING)]
        adacc = sb("adacc", [512])
        xT = sb("xT", [KT, S])
        hh = sb("hh", [KT, S], F32R)
        hl = sb("hl", [KT, S], F32R)
        oh = sb("oh", [KT, S], F32R)
        ol = sb("ol", [KT, S], F32R)
        pTh = sb("pTh", [2, S], F32R)
        pTl = sb("pTl", [2, S], F32R)
        con = sb("con", [CONST_N])
        trig = sb("trig", [3, 2, S])
        colsA = sb("colsA", [NROW_A])
        colsB = sb("colsB", [NROW_B])
        modT = sb("modT", [72])
        gain2 = sb("gain2", [24])
        small = sb("small", [64])
        ones1k = sb("ones1k", [P])
        ones128 = sb("ones128", [P])
        ones = sb("ones", [P])
        rootv = sb("rootv", [S])
        rstd = sb("rstd", [S])
        nb = sb("nb", [KT, S])
        SCR = 14400
        BF16 = mybir.dt.bfloat16
        zeros = sb('zeros', [P], BF16)
        negid = sb('negid', [P])
        scr = sb("scr", [SCR])

        def region():
            at = [0]

            def take(*shape):
                n = int(np.prod(shape))
                v = scr[:, at[0]:at[0] + n]
                at[0] += n
                assert at[0] <= SCR, at[0]
                if len(shape) == 2:
                    return v.rearrange("p (a b) -> p a b", b=shape[1])
                if len(shape) == 3:
                    return v.rearrange("p (a b c) -> p a b c", b=shape[1], c=shape[2])
                if len(shape) == 4:
                    return v.rearrange("p (a b c d) -> p a b c d", b=shape[1], c=shape[2], d=shape[3])
                return v
            return take

        psA = ps("psA", [4, 512])
        psX = ps("psX", [4, 512])
        psW = psX[:, 0:3, :]
        psS = psX[:, 3, :]
        accv = psA[:, :, :].rearrange("p a (b c) -> p (a b) c", b=2)

        def cst(name, n=None):
            at = CONST_AT[name]
            return con[:, at:at + (n or dict(CONST)[name])]

        ident = cst("ident")
        rotA, rotI, mean64 = cst("rotA"), cst("rotI"), cst("mean64")

        def colA(name, k=0, n=1):
            return colsA[:, COL_A[name] + k:COL_A[name] + k + n]

        def colB(name, k=0, n=1):
            return colsB[:, COL_B[name] + k:COL_B[name] + k + n]

        eps, zero, one, nlam = (small[:, i:i + 1] for i in range(4))
        halfpi = small[:, 4:5]
        omlb, lb = small[:, 8:16], small[:, 16:24]
        subg = small[:, 24:25]
        foxg_q, dsag_q = small[:, 25:26], small[:, 26:27]
        lamt = small[:, 28:32]
        condT = small[:, 32:40]
        ffb = small[0:8, 40:41]
        gmx, gex = small[:, 41:49], small[:, 48:64]

        take = region()
        xtok = take(TT, D)
        ptok = take(TT, S)
        rowsA, rowsB = take(P), take(P)
        posi = take(3, S)
        ang, kr, red = take(3, S), take(3, S), take(3, S)
        lamr = take(4, 64)
        lamp = take(2, 64)

        take = region()
        qT, kT = take(4, S), take(4, S)
        dvt, hvt = take(TT, 512), take(TT, 512)
        hqT, gT = take(4, S), take(4, S)
        lf = take(8, S)
        kin = nb
        E = take(8, TT, 129)
        qk = [take(2, 1024) for _ in range(2)]
        AT = lf.rearrange("p (t h) s -> p t h s", t=TT)
        at_qk = [q.rearrange("p a b -> p (a b)") for q in qk]
        da_p = [at_qk[0][:, 512 * i:512 * i + 512].rearrange("p (m k) -> p m k", m=2) for i in range(2)]
        da_w = [at_qk[0][:, 1024 + 512 * i:1536 + 512 * i].rearrange("p (k q) -> p k q", k=2)
                for i in range(2)]
        da_d = [at_qk[1][:, 256 * i:256 * i + 256].rearrange("p (m q) -> p m q", m=2) for i in range(2)]
        da_s = at_qk[1][:, 512:640]
        rot1 = at_qk[1][:, 1024:1536]
        hn_sq = at_qk[0].rearrange("p (h s) -> p h s", h=8)[:, 0:4]
        hn_rt = at_qk[0].rearrange("p (h s) -> p h s", h=8)[:, 4:8]
        hn_of = at_qk[1].rearrange("p (h s) -> p h s", h=8)[:, 0:4]

        take = region()
        f_t, f_g, f_a = take(2, S), take(2, S), take(2, S)
        f_s = take(2, 512)
        adar = [take(4, 512) for _ in range(2)]

        take = region()
        fqT, fkT, dqT = take(4, S), take(4, S), take(4, S)
        fvt = take(TT, 512)
        dkT, ikT, iqT = take(S), take(S), take(2, S)
        dvt2, iwt = take(TT, 64), take(TT, 8)
        gaS, gbS = take(KT, S), take(KT, S)
        Fc = take(S)
        m_sq, m_rt, m_xn = take(512), take(512), take(512)
        m_p = [take(384) for _ in range(2)]
        m_w = [take(384) for _ in range(2)]
        lgs = [m_w[0][:, 0:S], m_w[1][:, 0:S], m_p[0][:, 0:S]]
        m_d = [take(2, P) for _ in range(2)]
        m_s = take(160)
        sc0, sc1 = take(P), take(S)
        top8 = take(8)
        reluv = nb[:, :, :].rearrange("p a b -> p (a b)")
        mg = m_sq.rearrange("p (a s) -> p a s", a=2)

        block = ctx.enter_context(nc.Block())

        def chunk_src(w, c0, cols=256):
            return w.rearrange("(k p) n -> p k n", p=P)[:, :, c0:c0 + cols]

        def kview(buf, k):
            return buf[:, :].rearrange("p (k n) -> p k n", k=k)

        sp_, pe_ = nc.sync, nc.tensor


        @block.sync
        def _(sp):
            def load(b, srcs, i=0):
                if b >= RING:
                    sp.wait_ge(sem("lo_ready"), b - 2 + 3 * i)
                for n, (dst, src) in enumerate(srcs):
                    sp.dma_start(dst, src).then_inc(sem(f"raw{b % 3}"), 16)

            def cols(b, w, c0):
                return [(kview(raw[b % 3], KT), chunk_src(w, c0))]

            def rows2(b, w, r0):
                return [(kview(raw[b % 3], 2), w[bass.ds(r0, 256), :].rearrange("(k p) n -> p k n", p=P))]

            def coldyn(b, w, c0):
                return [(kview(raw[b % 3], KT), w.rearrange("(k p) n -> p k n", p=P)[:, :, bass.ds(c0, 256)])]

            small_load = sem("small_loaded")
            sp.dma_start(xtok, A["x"][0].rearrange("(t p) d -> p t d", p=P)).then_inc(sem("x_loaded"), 16)
            sp.dma_start(con[:, :], A["consts"]).then_inc(sem("con_loaded"), 16)
            n = 0
            rows = {
                "conv_w": A["ffn_conv_w"][0].rearrange("j (k p) -> (j k) p", p=P),
                "conv_b": A["ffn_conv_b"][0].rearrange("(k p) -> k p", p=P),
                "norm_mix": A["norm_mix_g"][0].rearrange("(k p) -> k p", p=P),
                "norm_ffn": A["norm_ffn_g"][0].rearrange("(k p) -> k p", p=P),
                "norm_ple": A["norm_ple_g"][0].rearrange("(k p) -> k p", p=P),
                "final": A["final_norm_g"].rearrange("(k p) -> k p", p=P),
                "subln": A["da_subln_g"], "hgnorm": A["hg_norm_g"],
                "ada_b": A["ada_b_2"][0].rearrange("(k p) -> k p", p=P),
                "norm_g": A["norm_g_2"][0].rearrange("j (k p) -> (j k) p", p=P),
                "c": A["c_2"][0].rearrange("(k p) -> k p", p=P),
                "gamma": A["hg_lb_gamma"].rearrange("z l (h p) -> (z l h) p", p=P),
            }
            for table, at, dst in ((ROWS_A, COL_A, rowsA), (ROWS_B, COL_B, rowsB)):
                for name, cnt in table:
                    if name in rows:
                        sp.dma_start(dst[at[name]:at[name] + cnt, :], rows[name]).then_inc(small_load, 16)
            for name, key in (("foxg", "fox_qk_g_2"), ("dsag", "dsa_qk_g_2")):
                a = COL_B[name]
                for half in range(2):
                    sp.dma_start(rowsB[a:a + 2, 64 * half:64 * half + 64], A[key][0]).then_inc(small_load, 16)
            load(0, cols(0, A["w_in"][0], IN1_COLS[0][1]))
            sp.dma_start(posi[:, 0, :].bitcast(I32), A["positions"][0].partition_broadcast(P)).then_inc(sem("pos_loaded"), 16)
            for j in (1, 2):
                sp.dma_start(posi[:, j, :].bitcast(I32), A["positions_2"][0].partition_broadcast(P)).then_inc(sem("pos_loaded"), 16)
            for j, name in enumerate(("lam_q1", "lam_k1", "lam_q2", "lam_k2")):
                sp.dma_start(lamr[:, j, :], A[name][0].partition_broadcast(P)).then_inc(sem("pos_loaded"), 16)
            sp.dma_start(ffb, A["fox_f_bias_2"].rearrange("a h -> h a")).then_inc(sem("pos_loaded"), 16)
            load(1, cols(1, A["w_in"][0], IN1_COLS[1][1]))
            sp.dma_start(ptok, A["p"][0, 0].rearrange("(t p) d -> p t d", p=P)).then_inc(sem("p_loaded"), 16)
            for j in range(2, 16):
                load(j, cols(j, A["w_in"][0], IN1_COLS[j][1]))
            for j in range(4):
                load(OUT1 + j, cols(OUT1 + j, A["w_out"][0], 256 * j))

            def ada(g, r, first=False):
                if not first:
                    sp.wait_ge(sem("ada_used"), 2 * g + r)
                sp.dma_start(adar[r][:, :, :], A["ada_w_2"][0].rearrange("(k p) n -> p k n", p=P)[
                    :, 4 * r:4 * r + 4, bass.ds(512 * g, 512)]).then_inc(sem(f"ada{r}_loaded"), 16)

            def ffn(b, w1, w3, w2, ada0):
                if ada0 == 0:
                    sp.wait_ge(sem("x_ready"), 3)
                    ada(0, 0, True)
                load(b, cols(b, w1, 0))
                load(b + 1, cols(b + 1, w3, 0))
                with sp.Fori(0, 9) as i:
                    load(b + 2, coldyn(b + 2, w1, 256 * i + 256), i)
                    if ada0 is not None:
                        ada(ada0 + i, 1)
                    load(b + 3, coldyn(b + 3, w3, 256 * i + 256), i)
                    load(b + 4, rows2(b + 4, w2, 256 * i), i)
                    if ada0 is not None:
                        ada(ada0 + 1 + i, 0)
                last = FSTEP - 1
                load(b + 29, cols(b + 29, w1, 256 * last))
                load(b + 30, cols(b + 30, w3, 256 * last))
                load(b + 31, [(kview(raw[(b + 31) % 3], 2), w2[256 * last - 256:256 * last, :].rearrange("(k p) n -> p k n", p=P))])
                load(b + 32, [(kview(raw[(b + 32) % 3], 2), w2[256 * last:256 * last + 256, :].rearrange("(k p) n -> p k n", p=P))])

            ffn(FFN1, A["w_ffn_gate"][0], A["w_ffn_up"][0], A["w_ffn_down"][0], 0)
            load(PLE, [(kview(raw[PLE % 3], 2), A["w_ple"][0].rearrange("(k p) n -> p k n", p=P))])
            for j in range(4):
                load(PGATE + j, cols(PGATE + j, A["w_ple_gate"][0], 256 * j))
            w1, w3, w2 = (A[f"ffn1_{w}_2"][0] for w in ("w1", "w3", "w2"))
            b = FFN2
            load(b, cols(b, w1, 0))
            load(b + 1, cols(b + 1, w3, 0))
            with sp.Fori(0, 8) as i:
                load(b + 2, coldyn(b + 2, w1, 256 * i + 256), i)
                ada(9 + i, 1)
                load(b + 3, coldyn(b + 3, w3, 256 * i + 256), i)
                load(b + 4, rows2(b + 4, w2, 256 * i), i)
                ada(10 + i, 0)
            for i in (8, 9):
                load(b + 2 + 3 * i, cols(b + 2 + 3 * i, w1, 256 * (i + 1)))
                if i == 8:
                    ada(17, 1)
                load(b + 3 + 3 * i, cols(b + 3 + 3 * i, w3, 256 * (i + 1)))
                load(b + 4 + 3 * i, [(kview(raw[(b + 4 + 3 * i) % 3], 2), w2[256 * i:256 * i + 256, :].rearrange("(k p) n -> p k n", p=P))])
            load(b + 32, [(kview(raw[(b + 32) % 3], 2), w2[2560:2816, :].rearrange("(k p) n -> p k n", p=P))])
            wi = A["w_in_2"][0]
            for j, (what, c0) in enumerate(IN2_COLS):
                n = IN2 + j
                if what == "misc":
                    load(n, [(kview(raw[n % 3], KT)[:, :, at:at + w], chunk_src(wi, c, w)) for at, c, w in MISC[c0]])
                else:
                    load(n, cols(n, wi, c0))
            for j in range(4):
                w = A["w_br_fox_2" if j % 2 == 0 else "w_br_dsa_2"][0]
                load(BRANCH + j, [(kview(raw[(BRANCH + j) % 3], 4), chunk_src(w, 512 * (j // 2), 512))])
            for j in range(4):
                load(OUT2 + j, cols(OUT2 + j, A["w_out_2"][0], 256 * j))
            ffn(FFN3, *(A[f"ffn2_{w}_2"][0] for w in ("w1", "w3", "w2")), None)
            o_v = out[0].rearrange("(t p) d -> p t d", p=P)
            for t in range(TT):
                sp.wait_ge(sem("out_ready"), t + 1)
                sp.dma_start(o_v[:, t, :], xtok[:, t, :]).then_inc(sem("stored"), 16)
            sp.wait_ge(sem("stored"), 32)

        def raw_count(b, i=0):
            extra = sum(len(MISC[m]) - 1 for m in range(2) if b >= IN2 + 6 + m and (b - IN2 - 6 - m) % 3 == 0)
            return 16 * (b // 3 + 1 + extra) + 16 * i


        @block.scalar
        def _(act):
            a_ = nc.scalar

            def hi(b, i=0):
                if b >= CHUNKS:
                    return
                act.wait_ge(sem(f"raw{b % 3}"), raw_count(b, i))
                if b >= RING:
                    act.wait_ge(sem("wt_used"), b - 2 + 3 * i)
                a_.copy(whi[b % 3][:, :], raw[b % 3][:, :]).then_inc(sem("hi_ready"), 1)

            def norm(m, need, p, shift):
                act.wait_ge(sem("x_ready"), need)
                for half in range(2):
                    v = slice(4 * half, 4 * half + 4)
                    a_.activation(nb[:, v, :], xT[:, v, :], ACT.Square).then_inc(sem("sq_ready"), 1)
                act.wait_ge(sem("mean_ready"), m + 1)
                a_.activation(rootv[:, :], psS[:, 0:S], ACT.Sqrt, bias=eps).then_inc(sem("root_ready"), 1)
                if p is None:
                    return
                for k in range(KT):
                    act.wait_ge(sem("hs_ready"), KT * p + k + 1)
                    a_.activation(hh[:, k, :], nb[:, k, :], ACT.Identity,
                                  bias=shift(k)).then_inc(sem("hhi_ready"), 1)

            act.wait_ge(sem("x_tr"), 1)
            act.wait_ge(sem("small_set"), 1)
            a_.copy(xT[:, 4:8, :], accv[:, 4:8, :]).then_inc(sem("x_copy"), 1)
            hi(0)
            hi(1)
            norm(0, 2, 0, lambda k: zero)
            act.wait_ge(sem("p_tr"), 1)
            a_.copy(pTh[:, :, :], psW[:, 2, :].rearrange("p (k s) -> p k s", k=2)).then_inc(sem("p_hi"), 1)
            act.wait_ge(sem("reduced"), 1)
            a_.activation(trig[:, :, 1, :], red, ACT.Sin).then_inc(sem("act_set"), 1)
            a_.activation(kr, red, ACT.Abs).then_inc(sem("act_set"), 1)
            act.wait_ge(sem("act_set"), 2)
            a_.activation(trig[:, :, 0, :], kr, ACT.Sin, bias=halfpi, scale=-1.0).then_inc(sem("act_set"), 1)
            act.wait_ge(sem("cols_ready"), 1)
            a_.activation(condT, colB("c", 0, 8), ACT.Silu).then_inc(sem("act_set"), 1)
            act.wait_ge(sem("gam_ready"), 1)
            a_.activation(gex, gex, ACT.Exp).then_inc(sem("act_set"), 1)
            act.wait_ge(sem("lam_ready"), 2)
            a_.activation(lamt[:, 2:4], lamt[:, 0:2], ACT.Exp).then_inc(sem("act_set"), 1)

            for j, (what, c0) in enumerate(IN1_COLS):
                hi(IN1 + j + 2)
                bank = psW[:, j % 3, :]
                half = (j % 2) * 2
                two = bank.rearrange("p (a s) -> p a s", a=2)
                act.wait_ge(sem("wt_used"), IN1 + j + 1)
                if j == 0:
                    act.wait_ge(sem("setup_done"), 1)
                if what in ("zf", "zb"):
                    d = (4 if what == "zb" else 0) + half
                    a_.activation(lf[:, d:d + 2, :], two, ACT.Sigmoid).then_inc(sem("sg_ready"), 1)
                    a_.activation(kin[:, d:d + 2, :], two, ACT.Sigmoid, scale=-1.0).then_inc(sem("in1_read_act"), 1)
                elif what == "g":
                    a_.activation(gT[:, half:half + 2, :], two, ACT.Sigmoid).then_inc(sem("gsig_ready"), 1)
                elif what == "hv":
                    a_.copy(hvt[:, :, (j % 2) * 256:(j % 2) * 256 + 256], two).then_inc(sem("in1_read_act"), 1)
                elif what in ("dq", "dk"):
                    a_.copy((qT if what == "dq" else kT)[:, half:half + 2, :], two).then_inc(sem("in1_read_act"), 1)
                elif what == "dv":
                    a_.copy(dvt[:, :, (j % 2) * 256:(j % 2) * 256 + 256], two).then_inc(sem("in1_read_act"), 1)

            act.wait_ge(sem("in1_read_act"), 4)
            act.wait_ge(sem("sg_ready"), 4)
            act.wait_ge(sem("lb_ready"), 1)
            for d in range(8):
                a_.activation(lf[:, d, :], lf[:, d, :], ACT.Ln, bias=lb[:, d:d + 1],
                              scale=omlb[:, d:d + 1]).then_inc(sem("lf_ready"), 1)
            for n in range(len(LEVELS) + 1):
                act.wait_ge(sem("lev_diff"), n + 1)
                a_.activation(qk[n % 2], qk[n % 2], ACT.Exp).then_inc(sem("lev_exp"), 1)
            def head_norm(tag, src, step, o_ready, per_half):
                for half in range(2):
                    act.wait_ge(sem(o_ready), per_half * (half + 1))
                    a_.activation(hn_sq[:, 2 * half:2 * half + 2, :], src(half), ACT.Square).then_inc(sem(f"{tag}_sq"), 1)
                for half in range(2):
                    act.wait_ge(sem(f"{tag}_mean"), half + 1)
                    a_.activation(hn_rt[:, 2 * half:2 * half + 2, :], psA[:, half, :].rearrange("p (a s) -> p a s", a=2),
                                  ACT.Sqrt, bias=eps).then_inc(sem(f"{tag}_root"), 1)
                for half in range(2):
                    act.wait_ge(sem(f"{tag}_of"), half + 1)
                    at = step + 2 * half
                    a_.copy(oh[:, at:at + 2, :], hn_of[:, 2 * half:2 * half + 2, :]).then_inc(sem(f"{tag}_ohi"), 1)

            head_norm("hg", lambda h: psW[:, h, :].rearrange("p (a s) -> p a s", a=2), 4, "hg_o", 1)

            for n in range(8):
                h, qt = n // 2, n % 2
                act.wait_ge(sem("da_max"), n + 1)
                if n >= 2:
                    act.wait_ge(sem("da_pt"), n - 1)
                for m in range(2):
                    a_.activation(da_p[n % 2][:, m, :], psX[:, 2 * (n % 2) + m, 0:256], ACT.Exp,
                                  bias=da_s[:, 16 + 2 * n + m:17 + 2 * n + m], scale=0.125,
                                  accum_out=da_s[:, 32 + 2 * n + m:33 + 2 * n + m]).then_inc(sem("da_exp"), 1)
                act.wait_ge(sem("da_pt"), n + 1)
                if h >= 2:
                    act.wait_ge(sem("da_oh"), h - 1)
                a_.copy(da_w[h % 2][:, :, P * qt:P * qt + P],
                        psA[:, n % 2, 0:256].rearrange("p (k q) -> p k q", k=2)).then_inc(sem("da_wt"), 1)
            head_norm("da", lambda h: psA[:, 2 + h, :].rearrange("p (a s) -> p a s", a=2), 0, "da_oh", 2)
            for j in range(4):
                hi(OUT1 + j + 2)

            def ffn(b, f, glu):
                def gate(nb_, i, first):
                    hi(nb_ + 2, i)
                    if glu:
                        act.wait_ge(sem("conv_ready"), FSTEP * f + 1 + i + first)
                    else:
                        act.wait_ge(sem("wt_used"), nb_ + 1 + 3 * i)
                    if f > 0 or first:
                        act.wait_ge(sem("actf_ready"), FSTEP * f + i + first)
                    if glu:
                        a_.activation(f_g, f_t, ACT.Gelu).then_inc(sem("ge_ready"), 1)
                    else:
                        a_.activation(f_g, psW[:, 0, :].rearrange("p (a s) -> p a s", a=2), ACT.Silu).then_inc(sem("ge_ready"), 1)

                def down(nb_, i, first):
                    hi(nb_ + 2, i)
                    act.wait_ge(sem("actf_ready"), FSTEP * f + 1 + i + first)
                    act.wait_ge(sem("wt_used"), nb_ + 1 + 3 * i)
                    a_.copy(oh[:, 0:2, :], f_a).then_inc(sem("fhi_ready"), 1)

                gate(b, 0, 0)
                hi(b + 3)
                act.wait_ge(sem("actf_ready"), FSTEP * f + 1)
                a_.copy(oh[:, 0:2, :], f_a).then_inc(sem("fhi_ready"), 1)
                loops = [(9, 0)] if f != 1 else [(8, 0), (1, 8)]
                for cnt, i0 in loops:
                    bb = b + 2 + 3 * i0
                    if cnt > 1:
                        with act.Fori(0, cnt) as i:
                            gate(bb, i, i0 + 1)
                            hi(bb + 3, i)
                            down(bb + 2, i, i0 + 1)
                    else:
                        gate(bb, 0, i0 + 1)
                        hi(bb + 3)
                        down(bb + 2, 0, i0 + 1)
                gate(b + 29, 0, 10)
                hi(b + 32)
                down(b + 31, 0, 10)
                hi(b + 34)

            norm(1, 6, 1, lambda k: zero)
            a_.preload_act_table(ACT.Gelu)
            ffn(FFN1, 0, True)
            norm(2, 8, 2, lambda k: zero)
            hi(PLE + 2)
            for j in range(4):
                hi(PGATE + j + 2)
                act.wait_ge(sem("wt_used"), PGATE + j + 1)
                if j >= 2:
                    act.wait_ge(sem("x_ready"), 8 + j - 1)
                a_.activation(f_s[:, j % 2, :], psW[:, j % 3, :], ACT.Sigmoid).then_inc(sem("pg_sig"), 1)
            norm(3, 12, None, None)
            norm(4, 20, 3, lambda k: modT[:, k:k + 1])
            a_.preload_act_table(ACT.Silu)
            ffn(FFN2, 1, False)
            norm(5, 28, 4, lambda k: modT[:, 24 + k:25 + k])

            def head_rms(n, width, post=None):
                act.wait_ge(sem("m_mean"), n + 1)
                if n:
                    act.wait_ge(sem("in2_read_dve"), n)
                a_.activation(m_rt[:, 0:width], psS[:, 0:width], ACT.Sqrt, bias=eps).then_inc(sem("m_root"), 1)

            for j, (what, c0) in enumerate(IN2_COLS):
                hi(IN2 + j + 2)
                if 1 <= j <= 7:
                    head_rms(j - 1, 256 if j == 7 else 512)
                act.wait_ge(sem("wt_used"), IN2 + j + 1)
                bank = psW[:, j % 3, :]
                two = bank.rearrange("p (a s) -> p a s", a=2)
                if what in ("fq", "fk", "dq") or (what, c0) == ("misc", 0):
                    w = 256 if what == "misc" else 512
                    if j >= 1:
                        act.wait_ge(sem("m_mean"), j)
                    a_.activation(m_sq[:, 0:w], bank[:, 0:w], ACT.Square).then_inc(sem("m_sq"), 1)
                    if what == "misc":
                        a_.copy(ikT, bank[:, 256:512]).then_inc(sem("misc_act"), 1)
                elif what == "misc":
                        a_.copy(iwt, psA[:, 1, 0:16].rearrange("p (t c) -> p t c", t=2)).then_inc(sem("misc_act"), 1)
                        a_.copy(dvt2, psA[:, 1, 128:256].rearrange("p (t c) -> p t c", t=2)).then_inc(sem("misc_act"), 1)
                elif what == "iq":
                    a_.copy(iqT, two).then_inc(sem("in2_read_act"), 1)
                elif what == "fv":
                    a_.copy(fvt[:, :, c0 - 1024:c0 - 768], two).then_inc(sem("in2_read_act"), 1)
                elif what in ("ga", "gb"):
                    k = 2 * ((j - 11) % 4)
                    a_.activation((gaS if what == "ga" else gbS)[:, k:k + 2, :], two, ACT.Sigmoid).then_inc(sem("in2_read_act"), 1)
            act.wait_ge(sem("ff_x"), 1)
            a_.activation(lgs[1][0:8, :], lgs[0][0:8, :], ACT.Abs).then_inc(sem("ff_act"), 1)
            act.wait_ge(sem("ff_act"), 1)
            a_.activation(lgs[1][0:8, :], lgs[1][0:8, :], ACT.Exp, scale=-1.0).then_inc(sem("ff_act"), 1)
            act.wait_ge(sem("ff_act"), 2)
            a_.activation(lgs[1][0:8, :], lgs[1][0:8, :], ACT.Ln, bias=one[0:8, :]).then_inc(sem("ff_act"), 1)

            def softmax_heads(tag, base):
                for h in range(8):
                    for qt in range(2):
                        act.wait_ge(sem(f"{tag}_max"), 2 * h + qt + 1)
                        if h >= 2:
                            act.wait_ge(sem(f"{tag}_pt"), h - 1)
                        v = m_p[h % 2][:, 0:128] if qt == 0 else m_p[h % 2][:, 128:384]
                        c = 2 * h + qt
                        a_.activation(v, v, ACT.Exp, bias=m_s[:, 32 + c:33 + c], scale=1.0,
                                      accum_out=m_s[:, 64 + c:65 + c]).then_inc(sem(f"{tag}_exp"), 1)
                    act.wait_ge(sem(f"{tag}_pt"), h + 1)
                    if h >= 2:
                        act.wait_ge(sem(f"{tag}_pv"), h - 1)
                    a_.copy(m_w[h % 2], psA[:, h % 2, 0:384]).then_inc(sem(f"{tag}_wt"), 1)
                for c in range(2):
                    act.wait_ge(sem(f"{tag}_pv"), 4 * c + 4)
                    dst = slice(4 * base + 2 * c, 4 * base + 2 * c + 2)
                    a_.copy(oh[:, dst, :], psA[:, 2 + c, :].rearrange("p (a s) -> p a s", a=2)).then_inc(sem(f"{tag}_ohi"), 1)

            softmax_heads("fox", 0)
            scale_i = 32 ** -0.5
            for qt in range(2):
                act.wait_ge(sem("ix_dots"), qt + 1)
                if qt == 1:
                    act.wait_ge(sem("ix_sum"), 1)
                w = 2 * P * (qt + 1)
                a_.activation(reluv[:, 0:4 * w].rearrange("p (a b) -> p a b", a=4), psA[:, :, 0:w], ACT.Relu,
                              scale=scale_i).then_inc(sem("ix_relu"), 1)
            softmax_heads("dsa", 1)

            for c in range(2):
                hi(BRANCH + 2 * c + 2)
                hi(BRANCH + 2 * c + 3)
                for t in range(2):
                    act.wait_ge(sem("mg_ready"), 2 * c + t + 1)
                    k = 4 * c + 2 * t
                    a_.copy(hh[:, k:k + 2, :], mg).then_inc(sem("mg_hi"), 1)
            for j in range(4):
                hi(OUT2 + j + 2)
            norm(6, 36, 5, lambda k: modT[:, 48 + k:49 + k])
            a_.preload_act_table(ACT.Silu)
            ffn(FFN3, 2, False)
            act.wait_ge(sem("out_tr"), 1)
            a_.copy(xtok[:, 0, :], psA[:, 0:2, :].rearrange("p a b -> p (a b)")).then_inc(sem("out_ready"), 1)
            act.wait_ge(sem("out_tr"), 2)
            a_.copy(xtok[:, 1, :], psA[:, 2:4, :].rearrange("p a b -> p (a b)")).then_inc(sem("out_ready"), 1)


        @block.vector
        def _(dve):
            v_ = nc.vector
            chain = [0, 0, 0]

            def link(ins):
                chain[0] += 1
                ins.then_inc(sem("dve_link"), 1)
                dve.wait_ge(sem("dve_link"), chain[0] + chain[1] * chain[2])

            def lo(b, i=0):
                if b >= CHUNKS:
                    return
                dve.wait_ge(sem("hi_ready"), b + 1 + 3 * i)
                v_.tensor_tensor(wlo[b % 3][:, :], raw[b % 3][:, :], whi[b % 3][:, :].bitcast(F32),
                                 ALU.subtract).then_inc(sem("lo_ready"), 1)

            def norm(m, p, gain, shift):
                dve.wait_ge(sem("root_ready"), m + 1)
                link(v_.reciprocal(rstd[:, :], rootv[:, :]))

                def low(k):
                    dve.wait_ge(sem("hhi_ready"), KT * p + k + 1)
                    v_.scalar_tensor_tensor(hl[:, k, :], nb[:, k, :], shift(k), hh[:, k, :].bitcast(F32),
                                            ALU.add, ALU.subtract).then_inc(sem("hlo_ready"), 1)

                for k in range(KT):
                    dst, s = (nb, "hs_ready") if p is not None else (xT, "x_ready")
                    v_.scalar_tensor_tensor(dst[:, k, :], xT[:, k, :], gain(k), rstd[:, :],
                                            ALU.mult, ALU.mult).then_inc(sem(s), 1)
                    if p is not None and k:
                        low(k - 1)
                if p is not None:
                    low(KT - 1)

            v_.memset(ones1k[:, :], 1.0 / D)
            v_.memset(ones128[:, :], 1.0 / P)
            v_.memset(ones[:, :], 1.0)
            v_.memset(zero, 0.0)
            v_.memset(zeros[:, :], 0.0)
            v_.memset(one, 1.0).then_inc(sem("ada_used"), 1)
            v_.memset(halfpi, float(np.pi / 2)).then_inc(sem("mod_ready"), 1)
            v_.memset(eps, EPS).then_inc(sem("small_set"), 1)
            dve.wait_ge(sem("cols_tr"), 1)
            v_.tensor_copy(colsA[:, :], psS[:, 0:NROW_A])
            v_.tensor_copy(colsB[:, :], psS[:, P:P + NROW_B]).then_inc(sem("cols_ready"), 1)
            dve.wait_ge(sem("x_tr"), 1)
            v_.tensor_copy(xT[:, 0:4, :], accv[:, 0:4, :]).then_inc(sem("x_ready"), 1)
            dve.wait_ge(sem("x_copy"), 1)
            dve.wait_ge(sem("cols_ready"), 1)
            v_.tensor_scalar(subg, colA("subln"), 1.0 - LAMBDA_INIT, None, ALU.mult).then_inc(sem("x_ready"), 1)
            lo(0)
            lo(1)
            norm(0, 0, lambda k: colA("norm_mix", k), lambda k: zero)
            v_.tensor_scalar(foxg_q, colB("foxg"), 0.125, None, ALU.mult)
            v_.tensor_scalar(dsag_q, colB("dsag"), 0.125, None, ALU.mult)
            dve.wait_ge(sem("p_hi"), 1)
            v_.tensor_tensor(pTl[:, :, :], psW[:, 2, :].rearrange("p (k s) -> p k s", k=2), pTh[:, :, :].bitcast(F32),
                             ALU.subtract).then_inc(sem("p_lo"), 1)
            gm = colB("gamma", 0, 16).rearrange("p (z l h) -> p z l h", z=2, l=2)
            ge = gex.rearrange("p (z l h) -> p z l h", z=2, l=2)
            mx = small[:, 8:16].rearrange("p (z h) -> p z h", z=2)
            link(v_.tensor_tensor(mx, gm[:, :, 0, :], gm[:, :, 1, :], ALU.max))
            v_.tensor_tensor(ge[:, :, 0, :], gm[:, :, 0, :], mx, ALU.subtract)
            v_.tensor_tensor(ge[:, :, 1, :], gm[:, :, 1, :], mx, ALU.subtract).then_inc(sem("gam_ready"), 1)
            dve.wait_ge(sem("pos_loaded"), 128)
            link(v_.tensor_copy(ang, posi.bitcast(I32)))
            dve.wait_ge(sem("con_loaded"), 16)
            freq = cst("freq")
            v_.tensor_scalar(negid[:, :], ident, -1.0, None, ALU.mult)
            v_.tensor_scalar(ang[:, 0:2, :], ang[:, 0:2, :], freq[:, 0:1], None, ALU.mult)
            link(v_.tensor_scalar(ang[:, 2, :], ang[:, 2, :], freq[:, 1:2], None, ALU.mult))
            magic = 12582912.0
            link(v_.tensor_scalar(kr, ang, float(1 / (2 * np.pi)), magic, ALU.mult, ALU.add))
            link(v_.tensor_scalar(kr, kr, -magic, None, ALU.add))
            c1 = 6.28125
            c2 = float(np.float32(int((2 * np.pi - c1) * 2 ** 18) / 2 ** 18))
            c3 = float(np.float32(2 * np.pi - c1 - c2))
            link(v_.scalar_tensor_tensor(red, kr, -c1, ang, ALU.mult, ALU.add))
            link(v_.scalar_tensor_tensor(red, kr, -c2, red, ALU.mult, ALU.add))
            link(v_.scalar_tensor_tensor(red, kr, -c3, red, ALU.mult, ALU.add))
            v_.tensor_scalar(red, red, 3.1415925, -3.1415925, ALU.min, ALU.max).then_inc(sem("reduced"), 1)
            for j in range(2):
                v_.tensor_tensor_reduce(lamp[:, j, :], lamr[:, 2 * j, :], lamr[:, 2 * j + 1, :], 1.0, 0.0,
                                        ALU.mult, ALU.add, lamt[:, j:j + 1]).then_inc(sem("lam_ready"), 1)
            dve.wait_ge(sem("act_set"), 5)
            link(v_.tensor_tensor(mx, ge[:, :, 0, :], ge[:, :, 1, :], ALU.add))
            link(v_.reciprocal(mx, mx))
            lbv = lb.rearrange("p (z h) -> p z h", z=2)
            link(v_.tensor_tensor(lbv, ge[:, :, 0, :], mx, ALU.mult))
            v_.tensor_scalar(omlb, lb, -1.0, 1.0, ALU.mult, ALU.add).then_inc(sem("lb_ready"), 1)
            dve.wait_ge(sem("act_set"), 6)
            dve.wait_ge(sem("lb_ready"), 1)
            v_.scalar_tensor_tensor(nlam, lamt[:, 3:4], -LAMBDA_INIT, lamt[:, 2:3], ALU.add,
                                    ALU.subtract).then_inc(sem("setup_done"), 1)

            for j, (what, c0) in enumerate(IN1_COLS):
                lo(IN1 + j + 2)
                half = (j % 2) * 2
                two = psW[:, j % 3, :].rearrange("p (a s) -> p a s", a=2)
                if what == "g":
                    dve.wait_ge(sem("gsig_ready"), j % 2 + 1)
                    v_.tensor_tensor(gT[:, half:half + 2, :], gT[:, half:half + 2, :], two, ALU.mult).then_inc(sem("in1_read_dve"), 1)
                elif what == "hq":
                    dve.wait_ge(sem("wt_used"), IN1 + j + 1)
                    v_.tensor_copy(hqT[:, half:half + 2, :], two).then_inc(sem("in1_read_dve"), 1)

            dve.wait_ge(sem("in1_read_act"), 4)
            for d in range(8):
                v_.tensor_scalar(kin[:, d, :], kin[:, d, :], omlb[:, d:d + 1], None, ALU.mult)
            v_.memset(E[:, :, :, 0:1], 0.0)
            for d in range(8):
                dve.wait_ge(sem("lf_ready"), d + 1)
                for t in range(TT):
                    ins = v_.tensor_tensor_scan(E[:, d, t, 1:129], ones[:, :], lf[:, d, P * t:P * t + P], 0.0,
                                                ALU.mult, ALU.add)
            link(ins)
            Ef, Eb = E[:, 0:4], E[:, 4:8]
            qh = hqT.rearrange("p h (t s) -> p h t s", t=2)
            kf = kin[:, 0:4].rearrange("p h (t s) -> p h t s", t=2)
            kb = kin[:, 4:8].rearrange("p h (t s) -> p h t s", t=2)

            def qk_of(n):
                q, k = qk[n % 2][:, 0, :], qk[n % 2][:, 1, :]
                return (x.rearrange("p (h t s) -> p h t s", h=4, t=2) for x in (q, k))

            def diffs(n):
                if n >= 2:
                    dve.wait_ge(sem("lev_mm"), n - 1)
                if n == 0:
                    Q, K = qk_of(n)
                    tot_b = Eb[:, :, 0, 128:129].broadcast_to([P, 4, P])
                    tot_f = Ef[:, :, 0, 128:129].broadcast_to([P, 4, P])
                    v_.tensor_copy(Q[:, :, 1, :], Ef[:, :, 1, 1:129])
                    v_.tensor_tensor(Q[:, :, 0, :], tot_b, Eb[:, :, 0, 0:128], ALU.subtract)
                    v_.tensor_tensor(K[:, :, 0, :], tot_f, Ef[:, :, 0, 1:129], ALU.subtract)
                    v_.tensor_copy(K[:, :, 1, :], Eb[:, :, 1, 0:128]).then_inc(sem("lev_diff"), 1)
                    return
                B = LEVELS[n - 1]
                H = B // 2
                q, k = (qk[n % 2][:, i, :].rearrange("p (r b s) -> p r b s", r=8, s=B) for i in range(2))

                def rows(x, off):
                    return x.rearrange("p h t s -> p (h t) s")[:, :, off:off + P].rearrange("p r (b s) -> p r b s", s=B)

                f0, f1, b0 = rows(Ef, 0), rows(Ef, 1), rows(Eb, 0)
                nb_ = P // B
                for r in range(1):
                    mf = f0[:, :, :, H:H + 1].broadcast_to([P, 8, nb_, H])
                    mb = b0[:, :, :, H:H + 1].broadcast_to([P, 8, nb_, H])
                    v_.tensor_tensor(q[:, :, :, H:B], f1[:, :, :, H:B], mf, ALU.subtract)
                    v_.tensor_tensor(k[:, :, :, 0:H], mf, f1[:, :, :, 0:H], ALU.subtract)
                    v_.tensor_tensor(q[:, :, :, 0:H], mb, b0[:, :, :, 0:H], ALU.subtract)
                    v_.tensor_tensor(k[:, :, :, H:B], b0[:, :, :, H:B], mb, ALU.subtract).then_inc(sem("lev_diff"), 1)

            def scaled(n):
                dve.wait_ge(sem("lev_exp"), n + 1)
                if n == 0:
                    Q, K = qk_of(n)
                    v_.tensor_tensor(Q, Q, qh, ALU.mult)
                    v_.tensor_tensor(K[:, :, 0, :], K[:, :, 0, :], kf[:, :, 0, :], ALU.mult)
                    v_.tensor_tensor(K[:, :, 1, :], K[:, :, 1, :], kb[:, :, 1, :], ALU.mult).then_inc(sem("lev_qk"), 1)
                    return
                B = LEVELS[n - 1]
                H = B // 2
                q, k = (qk[n % 2][:, i, :].rearrange("p (r b s) -> p r b s", r=8, s=B) for i in range(2))
                qf = qk[n % 2][:, 0, :]
                v_.tensor_tensor(qf, qf, hqT.rearrange("p h s -> p (h s)"), ALU.mult)
                kfv, kbv = (x.rearrange("p h s -> p (h s)").rearrange("p (r b s) -> p r b s", r=8, s=B)
                            for x in (kin[:, 0:4], kin[:, 4:8]))
                v_.tensor_tensor(k[:, :, :, 0:H], k[:, :, :, 0:H], kfv[:, :, :, 0:H], ALU.mult)
                v_.tensor_tensor(k[:, :, :, H:B], k[:, :, :, H:B], kbv[:, :, :, H:B], ALU.mult).then_inc(sem("lev_qk"), 1)

            def place(n):
                dve.wait_ge(sem("lev_mm"), n + 1)
                for t in range(TT):
                    src = psA[:, 2 * (n % 2) + t, :].rearrange("p (h s) -> p h s", h=4)
                    if n == 0:
                        dst = AT[:, t, :, P * (1 - t):P * (1 - t) + P]
                    else:
                        dst = AT[:, t, :, P * t:P * t + P]
                    if n <= 1:
                        ins = v_.tensor_copy(dst, src)
                    else:
                        if n <= 7:
                            m = cst("levels")[:, (n - 2) * P:(n - 1) * P]
                        else:
                            m = ident
                        m = m.bitcast(I32).unsqueeze(1).broadcast_to([P, 4, P])
                        ins = v_.copy_predicated(dst, m, src)
                ins.then_inc(sem("lev_placed"), 1)
                dve.wait_ge(sem("lev_placed"), n + 1)

            nlev = len(LEVELS) + 2
            diffs(0)
            for n in range(nlev):
                if n + 1 < nlev - 1:
                    diffs(n + 1)
                if n < nlev - 1:
                    scaled(n)
                else:
                    dve.wait_ge(sem("lev_mm"), n - 1)
                    v_.tensor_tensor(qk[n % 2][:, 1, :], kin[:, 0:4].rearrange("p h s -> p (h s)"),
                                     kin[:, 4:8].rearrange("p h s -> p (h s)"), ALU.add).then_inc(sem("lev_qk"), 1)
                if n >= 1:
                    place(n - 1)
            place(nlev - 1)

            def head_norm(tag, src, gain, step, silu):
                for half in range(2):
                    hs = slice(2 * half, 2 * half + 2)
                    dve.wait_ge(sem(f"{tag}_root"), half + 1)
                    link(v_.reciprocal(hn_rt[:, hs, :], hn_rt[:, hs, :]))
                    ins = v_.scalar_tensor_tensor(hn_of[:, hs, :], src(half), gain, hn_rt[:, hs, :], ALU.mult, ALU.mult)
                    if silu:
                        link(ins)
                        ins = v_.tensor_tensor(hn_of[:, hs, :], hn_of[:, hs, :], gT[:, hs, :], ALU.mult)
                    ins.then_inc(sem(f"{tag}_of"), 1)
                for half in range(2):
                    dve.wait_ge(sem(f"{tag}_ohi"), half + 1)
                    at = step + 2 * half
                    v_.tensor_tensor(ol[:, at:at + 2, :], hn_of[:, 2 * half:2 * half + 2, :], oh[:, at:at + 2, :].bitcast(F32),
                                     ALU.subtract).then_inc(sem(f"{tag}_olo"), 1)

            head_norm("hg", lambda h: psW[:, h, :].rearrange("p (a s) -> p a s", a=2), colA("hgnorm"), 4, True)

            def rotary(dst, src, rot, table, width, tmp):
                c = trig[:, table, 0, :]
                s = trig[:, table, 1, :]
                if width == 2:
                    c, s = (x.unsqueeze(1).broadcast_to([P, 2, S]) for x in (c, s))
                link(v_.tensor_tensor(tmp, rot, s, ALU.mult))
                link(v_.tensor_tensor(dst, src, c, ALU.mult))
                return v_.tensor_tensor(dst, dst, tmp, ALU.add)

            for n in range(4):
                x = (qT if n < 2 else kT)[:, 2 * (n % 2):2 * (n % 2) + 2, :]
                dve.wait_ge(sem("rot1"), n + 1)
                if n:
                    dve.wait_ge(sem("rot1_done"), n)
                rotary(x, x, psW[:, n % 3, :].rearrange("p (a s) -> p a s", a=2), 0, 2,
                       rot1.rearrange("p (a s) -> p a s", a=2)).then_inc(sem("rot1_done"), 1)

            for n in range(8):
                dve.wait_ge(sem("da_sc"), n + 1)
                sc = psX[:, 2 * (n % 2):2 * (n % 2) + 2, 0:256]
                link(v_.tensor_reduce(da_s[:, 2 * n:2 * n + 2], sc, AXX, ALU.max))
                v_.tensor_scalar(da_s[:, 16 + 2 * n:18 + 2 * n], da_s[:, 2 * n:2 * n + 2], -0.125, None,
                                 ALU.mult).then_inc(sem("da_max"), 1)
                dve.wait_ge(sem("da_exp"), 2 * n + 2)
                link(v_.reciprocal(da_s[:, 48 + 2 * n:50 + 2 * n], da_s[:, 32 + 2 * n:34 + 2 * n]))
                if n >= 2:
                    dve.wait_ge(sem("da_pt"), n - 1)
                v_.tensor_scalar(da_d[n % 2][:, 0, :], ident, da_s[:, 48 + 2 * n:49 + 2 * n], None, ALU.mult)
                v_.tensor_scalar(da_d[n % 2][:, 1, :], ident, da_s[:, 49 + 2 * n:50 + 2 * n], nlam, ALU.mult,
                                 ALU.mult).then_inc(sem("da_diag"), 1)
            head_norm("da", lambda h: psA[:, 2 + h, :].rearrange("p (a s) -> p a s", a=2), subg, 0, False)

            for j in range(4):
                lo(OUT1 + j + 2)
                dve.wait_ge(sem("wt_used"), OUT1 + j + 1)
                x = xT[:, 2 * j:2 * j + 2, :]
                v_.tensor_tensor(x, x, psW[:, j % 3, :].rearrange("p (a s) -> p a s", a=2), ALU.add).then_inc(sem("x_ready"), 1)

            gatep = psW[:, 0, :].rearrange("p (a s) -> p a s", a=2)
            upp = psW[:, 1, :].rearrange("p (a s) -> p a s", a=2)

            def conv(f, nb_, i, first):
                dve.wait_ge(sem("wt_used"), nb_ + 1 + 3 * i)
                if first:
                    dve.wait_ge(sem("ge_ready"), FSTEP * f + i + first)
                for t in range(2):
                    def tap(j):
                        if isinstance(i, int):
                            return colsA[:, 22 * j + 2 * (i + first) + t:22 * j + 2 * (i + first) + t + 1]
                        return colsA[:, bass.ds(2 * i + (22 * j + 2 * first + t), 1)]
                    ft = f_t[:, t, :]
                    link(v_.tensor_scalar(ft, gatep[:, t, :], tap(1), tap(3), ALU.mult, ALU.add))
                    link(v_.scalar_tensor_tensor(ft[:, 1:S], gatep[:, t, 0:S - 1], tap(0), ft[:, 1:S], ALU.mult, ALU.add))
                    ins = v_.scalar_tensor_tensor(ft[:, 0:S - 1], gatep[:, t, 1:S], tap(2), ft[:, 0:S - 1], ALU.mult, ALU.add)
                ins.then_inc(sem("conv_ready"), 1)

            def ada_part(g, r):
                if isinstance(g, int) and g == 0:
                    dve.wait_ge(sem("act_set"), 4)
                dve.wait_ge(sem(f"ada{r}_loaded"), 16 * g + 16)
                if r == 0 and not (isinstance(g, int) and g == 0):
                    dve.wait_ge(sem("ada_sum"), g + 1)
                for k in range(4):
                    kk = 4 * r + k
                    if kk == 0:
                        ins = v_.tensor_scalar(adacc[:, :], adar[r][:, k, :], condT[:, kk:kk + 1], None, ALU.mult)
                    else:
                        ins = v_.scalar_tensor_tensor(adacc[:, :], adar[r][:, k, :], condT[:, kk:kk + 1], adacc[:, :],
                                                      ALU.mult, ALU.add)
                    if k < 3:
                        link(ins)
                ins.then_inc(sem("ada_used"), 1)
                dve.wait_ge(sem("ada_used"), 2 * g + r + 2)

            def ada_out(g):
                dve.wait_ge(sem("ada_sum"), g + 2)
                if isinstance(g, int):
                    dst, b = modT[:, 4 * g:4 * g + 4], colB("ada_b", 4 * g, 4)
                else:
                    dst, b = modT[:, bass.ds(4 * g, 4)], colsB[:, bass.ds(4 * g + COL_B["ada_b"], 4)]
                v_.tensor_tensor(dst, psS[:, 256:260], b, ALU.add).then_inc(sem("mod_ready"), 1)

            def hidden(f, nb_, i, first):
                dve.wait_ge(sem("wt_used"), nb_ + 1 + 3 * i)
                dve.wait_ge(sem("ge_ready"), FSTEP * f + 1 + i + first)
                if f > 0 or first:
                    dve.wait_ge(sem("flo_ready"), FSTEP * f + i + first)
                v_.tensor_tensor(f_a, f_g, upp, ALU.mult).then_inc(sem("actf_ready"), 1)

            def hidden_lo(f, i, first):
                dve.wait_ge(sem("fhi_ready"), FSTEP * f + 1 + i + first)
                dve.wait_ge(sem("actf_ready"), FSTEP * f + 1 + i + first)
                v_.tensor_tensor(ol[:, 0:2, :], f_a, oh[:, 0:2, :].bitcast(F32), ALU.subtract).then_inc(sem("flo_ready"), 1)

            def step(f, nb_, i, first, ada):
                lo(nb_ + 2, i)
                if f == 0:
                    conv(f, nb_, i, first)
                if ada is not None:
                    ada_part(ada + i, 0)
                lo(nb_ + 3, i)
                hidden(f, nb_ + 1, i, first)
                if ada is not None:
                    ada_part(ada + i, 1)
                lo(nb_ + 4, i)
                hidden_lo(f, i, first)
                if ada is not None:
                    ada_out(ada + i)

            def ffn(b, f, ada, gate):
                lo(b + 2)
                if f == 0:
                    conv(f, b, 0, 0)
                lo(b + 3)
                hidden(f, b + 1, 0, 0)
                hidden_lo(f, 0, 0)
                before = chain[0]
                chain[1] = (4 if f == 0 else 0) + (6 if ada is not None else 0)
                loops = [(9, 0)] if f != 1 else [(8, 0), (1, 8)]
                for cnt, i0 in loops:
                    bb = b + 2 + 3 * i0
                    g = None if ada is None else ada + i0
                    start = chain[0]
                    if cnt > 1:
                        with dve.Fori(0, cnt) as i:
                            chain[2] = i
                            step(f, bb, i, i0 + 1, g)
                        assert chain[0] - start == chain[1], (chain[0] - start, chain[1])
                        chain[0] = start + chain[1] * cnt
                        chain[2] = 0
                    else:
                        step(f, bb, 0, i0 + 1, g)
                step(f, b + 29, 0, 10, None)
                lo(b + 34)
                chain[1] = 0
                dve.wait_ge(sem("wt_used"), b + 33)
                if gate is None:
                    for c in range(2):
                        x = xT[:, 4 * c:4 * c + 4, :]
                        v_.tensor_tensor(x, x, accv[:, 4 * c:4 * c + 4, :], ALU.add).then_inc(sem("x_ready"), 1)
                else:
                    for k in range(KT):
                        v_.scalar_tensor_tensor(xT[:, k, :], accv[:, k, :], gate(k), xT[:, k, :], ALU.mult,
                                                ALU.add).then_inc(sem("x_ready"), 1)

            norm(1, 1, lambda k: colA("norm_ffn", k), lambda k: zero)
            ffn(FFN1, 0, 0, None)

            norm(2, 2, lambda k: colA("norm_ple", k), lambda k: zero)
            lo(PLE + 2)
            for j in range(4):
                lo(PGATE + j + 2)
                dve.wait_ge(sem("pg_sig"), j + 1)
                dve.wait_ge(sem("wt_used"), PLE + 1)
                v = slice(2 * j, 2 * j + 2)
                sg = f_s[:, j % 2, :].rearrange("p (a s) -> p a s", a=2)
                link(v_.tensor_tensor(sg, sg, accv[:, v, :], ALU.mult))
                v_.tensor_tensor(xT[:, v, :], xT[:, v, :], sg, ALU.add).then_inc(sem("x_ready"), 1)
            norm(3, None, lambda k: colA("final", k), None)

            def gains(s):
                dve.wait_ge(sem("mod_ready"), 19 if s else 10)
                v_.scalar_tensor_tensor(gain2[:, 8 * s:8 * s + 8], modT[:, 24 * s + 8:24 * s + 16], 1.0,
                                        colB("norm_g", 8 * s, 8), ALU.add, ALU.mult)
                gate = modT[:, 24 * s + 16:24 * s + 24]
                link(v_.tensor_scalar(gate, gate, 1.0 if s == 1 else 0.5, None, ALU.mult))

            gains(0)
            norm(4, 3, lambda k: gain2[:, k:k + 1], lambda k: modT[:, k:k + 1])
            ffn(FFN2, 1, 9, lambda k: modT[:, 16 + k:17 + k])
            gains(1)
            gains(2)
            norm(5, 4, lambda k: gain2[:, 8 + k:9 + k], lambda k: modT[:, 24 + k:25 + k])

            def normed(n):
                what = IN2_COLS[n][0]
                w = 256 if what == "misc" else 512
                dve.wait_ge(sem("m_root"), n + 1)
                link(v_.reciprocal(m_rt[:, 0:w], m_rt[:, 0:w]))
                gain = {"fq": foxg_q, "fk": colB("foxg", 1), "dq": dsag_q, "misc": colB("dsag", 1)}[what]
                dst = {"fq": fqT, "fk": fkT, "dq": dqT}.get(what)
                dst = dkT if dst is None else dst[:, 2 * (n % 2):2 * (n % 2) + 2, :].rearrange("p a s -> p (a s)")
                v_.scalar_tensor_tensor(dst, psW[:, n % 3, 0:w], gain, m_rt[:, 0:w], ALU.mult, ALU.mult).then_inc(sem("in2_read_dve"), 1)

            for j, (what, c0) in enumerate(IN2_COLS):
                lo(IN2 + j + 2)
                if 1 <= j <= 7:
                    normed(j - 1)
                if (what, c0) == ("misc", 1):
                    dve.wait_ge(sem("wt_used"), IN2 + j + 1)
                    v_.tensor_scalar(lgs[0][0:8, :], psA[0:8, 0, 0:S], ffb, None, ALU.add).then_inc(sem("ff_x"), 1)
            dve.wait_ge(sem("ff_x"), 1)
            link(v_.tensor_scalar(lgs[2][0:8, :], lgs[0][0:8, :], 0.0, None, ALU.min))
            dve.wait_ge(sem("ff_act"), 3)
            link(v_.tensor_tensor(lgs[2][0:8, :], lgs[2][0:8, :], lgs[1][0:8, :], ALU.subtract))
            link(v_.memset(Fc, 0.0))
            link(v_.tensor_tensor_scan(Fc[0:8, :], one[0:8, :].broadcast_to([8, S]), lgs[2][0:8, :], 0.0, ALU.mult, ALU.add))
            v_.tensor_copy(Fc[64:72, :], Fc[0:8, :]).then_inc(sem("F_ready"), 1)
            dve.wait_ge(sem("rot2"), 1)
            for n in range(2):
                x = dqT[:, 2 * n:2 * n + 2, :]
                link(rotary(x, x, psA[:, n, :].rearrange("p (a s) -> p a s", a=2), 1, 2,
                            m_xn.rearrange("p (a s) -> p a s", a=2)))
            link(rotary(iqT, iqT, psA[:, 2, :].rearrange("p (a s) -> p a s", a=2), 2, 2,
                        m_xn.rearrange("p (a s) -> p a s", a=2)))
            link(rotary(dkT, dkT, psA[:, 3, 0:S], 1, 1, m_xn[:, 0:S]))
            rotary(ikT, ikT, psA[:, 3, S:2 * S], 2, 1, m_xn[:, 0:S]).then_inc(sem("rot2_done"), 1)

            def softmax_heads(tag, bias0, bias1):
                for h in range(8):
                    dve.wait_ge(sem(f"{tag}_sc"), h + 1)
                    if h >= 2:
                        dve.wait_ge(sem(f"{tag}_pt"), h - 1)
                    bank = psW[:, h % 3, :]
                    for qt in range(2):
                        c = 2 * h + qt
                        v, s, b = (m_p[h % 2][:, 0:128], bank[:, 0:128], bias0) if qt == 0 else (
                            m_p[h % 2][:, 128:384], bank[:, 128:384], bias1)
                        link(v_.tensor_tensor_reduce(v, s, b, 1.0, -3e38, ALU.add, ALU.max, m_s[:, c:c + 1]))
                        v_.tensor_scalar(m_s[:, 32 + c:33 + c], m_s[:, c:c + 1], -1.0, None, ALU.mult).then_inc(sem(f"{tag}_max"), 1)
                    dve.wait_ge(sem(f"{tag}_exp"), 2 * h + 2)
                    link(v_.reciprocal(m_s[:, 96 + 2 * h:98 + 2 * h], m_s[:, 64 + 2 * h:66 + 2 * h]))
                    for qt in range(2):
                        ins = v_.tensor_scalar(m_d[h % 2][:, qt, :], ident, m_s[:, 96 + 2 * h + qt:97 + 2 * h + qt], None, ALU.mult)
                    ins.then_inc(sem(f"{tag}_diag"), 1)

            def out_lo(tag, base):
                for c in range(2):
                    dve.wait_ge(sem(f"{tag}_ohi"), c + 1)
                    dst = slice(4 * base + 2 * c, 4 * base + 2 * c + 2)
                    v_.tensor_tensor(ol[:, dst, :], psA[:, 2 + c, :].rearrange("p (a s) -> p a s", a=2),
                                     oh[:, dst, :].bitcast(F32), ALU.subtract).then_inc(sem(f"{tag}_olo"), 1)

            causal = cst("causal")
            softmax_heads("fox", causal[:, P:2 * P], causal)
            out_lo("fox", 0)

            dve.wait_ge(sem("misc_act"), 3)
            link(v_.tensor_scalar(iwt, iwt, 8 ** -0.5, None, ALU.mult))
            for qt in range(2):
                w = P * (qt + 1)
                sc = (sc0, sc1)[qt]
                dve.wait_ge(sem("ix_relu"), qt + 1)
                for h in range(8):
                    r = reluv[:, (h % 4) * 2 * w + (h // 4) * w:(h % 4) * 2 * w + (h // 4) * w + w]
                    if h == 0:
                        ins = v_.tensor_scalar(sc, r, iwt[:, qt, 0:1], None, ALU.mult)
                    else:
                        ins = v_.scalar_tensor_tensor(sc, r, iwt[:, qt, h:h + 1], sc, ALU.mult, ALU.add)
                    if h < 7:
                        link(ins)
                ins.then_inc(sem("ix_sum"), 1)
                dve.wait_ge(sem("ix_sum"), qt + 1)
                d = sc[:, w - P:w]
                link(v_.tensor_tensor(d, d, cst("admit")[:, P:2 * P], ALU.add))
                for _r in range(TOPK // 8):
                    link(v_.max(top8, sc))
                    link(v_.match_replace(sc, top8, sc, PICKED))
                ins = v_.tensor_scalar(sc, sc, 0.5 * PICKED, BIG, ALU.is_gt, ALU.mult)
                link(ins)
            softmax_heads("dsa", sc0, sc1)
            out_lo("dsa", 1)

            for c in range(2):
                lo(BRANCH + 2 * c + 2)
                lo(BRANCH + 2 * c + 3)
                dve.wait_ge(sem("wt_used"), BRANCH + 2 * c + 2)
                for t in range(2):
                    k = 4 * c + 2 * t
                    ya, yb = (psA[:, i + t, :].rearrange("p (a s) -> p a s", a=2) for i in (0, 2))
                    ga, gb = gaS[:, k:k + 2, :], gbS[:, k:k + 2, :]
                    v_.tensor_tensor(ga, ga, ya, ALU.mult)
                    link(v_.tensor_tensor(gb, gb, yb, ALU.mult))
                    if c or t:
                        dve.wait_ge(sem("mg_hi"), 2 * c + t)
                        dve.wait_ge(sem("mg_lo"), 2 * c + t)
                    v_.tensor_tensor(mg, ga, gb, ALU.add).then_inc(sem("mg_ready"), 1)
                    dve.wait_ge(sem("mg_hi"), 2 * c + t + 1)
                    dve.wait_ge(sem("mg_ready"), 2 * c + t + 1)
                    v_.tensor_tensor(hl[:, k:k + 2, :], mg, hh[:, k:k + 2, :].bitcast(F32),
                                     ALU.subtract).then_inc(sem("mg_lo"), 1)
            for j in range(4):
                lo(OUT2 + j + 2)
                dve.wait_ge(sem("wt_used"), OUT2 + j + 1)
                for t in range(2):
                    k = 2 * j + t
                    v_.scalar_tensor_tensor(xT[:, k, :], psW[:, j % 3, 256 * t:256 * t + 256], modT[:, 40 + k:41 + k],
                                            xT[:, k, :], ALU.mult, ALU.add).then_inc(sem("x_ready"), 1)
            norm(6, 5, lambda k: gain2[:, 16 + k:17 + k], lambda k: modT[:, 48 + k:49 + k])
            ffn(FFN3, 2, None, lambda k: modT[:, 64 + k:65 + k])


        @block.tensor
        def _(pe):
            def have(b, i=0):
                pe.wait_ge(sem("lo_ready"), b + 1 + 3 * i)

            def mm3(dst, ws, w, xh, xl, start, stop):
                wh, wl = (w(kview(b, ws[1])) for b in (whi[ws[0] % 3], wlo[ws[0] % 3]))
                pe.matmul(dst, wh, xh, start=start, stop=False, skip_group_check=True)
                pe.matmul(dst, wh, xl, start=False, stop=False, skip_group_check=True)
                return pe.matmul(dst, wl, xh, start=False, stop=stop, skip_group_check=True)

            def mm3t(dst, ws, w, xh, xl, start, stop):
                wh, wl = (w(kview(b, ws[1])) for b in (whi[ws[0] % 3], wlo[ws[0] % 3]))
                pe.matmul(dst, xh, wh, start=start, stop=False, skip_group_check=True)
                pe.matmul(dst, xh, wl, start=False, stop=False, skip_group_check=True)
                return pe.matmul(dst, xl, wh, start=False, stop=stop, skip_group_check=True)

            def gemm(b, bank, xh, xl, i=0, first=None, done="wt_used"):
                have(b, i)
                for t in range(2):
                    for k in range(KT):
                        if first is not None and t == 0:
                            pe.wait_ge(sem("hlo_ready"), KT * first + k + 1)
                        ins = mm3(bank[:, 256 * t:256 * t + 256], (b, KT), lambda w: w[:, k, P * t:P * t + P],
                                  xh[:, k, :], xl[:, k, :], k == 0, k == KT - 1)
                ins.then_inc(sem(done), 1)

            def gemm_tok(b, bank):
                have(b)
                for t in range(2):
                    for k in range(KT):
                        ins = mm3t(bank[:, 256 * t:256 * t + 256], (b, KT), lambda w: w[:, k, :],
                                   hh[:, k, P * t:P * t + P], hl[:, k, P * t:P * t + P], k == 0, k == KT - 1)
                ins.then_inc(sem("wt_used"), 1)

            def mean(m):
                for k in range(KT):
                    pe.wait_ge(sem("sq_ready"), 2 * m + k // 4 + 1)
                    ins = pe.matmul(psS[:, 0:S], ones1k[:, :], nb[:, k, :], start=(k == 0), stop=(k == KT - 1))
                ins.then_inc(sem("mean_ready"), 1)

            pe.wait_ge(sem("con_loaded"), 16)
            pe.wait_ge(sem("x_loaded"), 16)
            for k in range(KT):
                for t in range(TT):
                    ins = pe.transpose(accv[:, k, P * t:P * t + P], xtok[:, t, P * k:P * k + P], ident)
            ins.then_inc(sem("x_tr"), 1)
            pe.wait_ge(sem("small_loaded"), 16 * 16)
            pe.transpose(psS[:, 0:NROW_A], rowsA[0:NROW_A, :], ident[0:NROW_A, 0:NROW_A]).then_inc(sem("ada_sum"), 1)
            pe.transpose(psS[:, P:P + NROW_B], rowsB[0:NROW_B, :], ident[0:NROW_B, 0:NROW_B]).then_inc(sem("cols_tr"), 1)
            pe.wait_ge(sem("cols_ready"), 1)
            pe.wait_ge(sem("small_set"), 1)
            mean(0)
            pe.wait_ge(sem("p_loaded"), 16)
            for k in range(2):
                for t in range(TT):
                    ins = pe.transpose(psW[:, 2, 256 * k + P * t:256 * k + P * t + P], ptok[:, t, P * k:P * k + P], ident)
            ins.then_inc(sem("p_tr"), 1)

            for j, (what, c0) in enumerate(IN1_COLS):
                if j == 2:
                    pe.wait_ge(sem("p_lo"), 1)
                if j >= 3:
                    r = j - 3
                    if r < 4:
                        pe.wait_ge(sem("in1_read_act"), r + 1)
                    elif r < 8:
                        pe.wait_ge(sem("in1_read_dve"), r - 3)
                    else:
                        pe.wait_ge(sem("in1_read_act"), r - 3)
                if what in ("hv", "dv"):
                    gemm_tok(IN1 + j, psW[:, j % 3, :])
                else:
                    gemm(IN1 + j, psW[:, j % 3, :], hh, hl, first=0 if j == 0 else None)

            nlev = len(LEVELS) + 2
            for n in range(nlev):
                pe.wait_ge(sem("lev_qk"), n + 1)
                if n >= 2:
                    pe.wait_ge(sem("lev_placed"), n - 1)
                for t in range(TT):
                    for h in range(4):
                        k = qk[n % 2][:, 1, :].rearrange("p (h s) -> p h s", h=4)[:, h, P * t:P * t + P]
                        tq = 1 - t if n == 0 else t
                        q = (hqT if n == nlev - 1 else qk[n % 2][:, 0, :].rearrange("p (h s) -> p h s", h=4))[:, h, P * tq:P * tq + P]
                        ins = pe.matmul(psA[:, 2 * (n % 2) + t, P * h:P * h + P], k, q, start=True, stop=True,
                                        skip_group_check=True)
                ins.then_inc(sem("lev_mm"), 1)
            pe.wait_ge(sem("lev_placed"), nlev)
            pe.wait_ge(sem("in1_read_act"), 12)
            for h in range(4):
                for t in range(TT):
                    ins = pe.matmul(psW[:, h // 2, 256 * (h % 2):256 * (h % 2) + 256], hvt[:, t, P * h:P * h + P],
                                    AT[:, t, h, :], start=(t == 0 and h % 2 == 0), stop=(t == 1), skip_group_check=True)
                if h % 2:
                    ins.then_inc(sem("hg_o"), 1)

            def head_means(tag):
                for half in range(2):
                    pe.wait_ge(sem(f"{tag}_sq"), half + 1)
                    pe.matmul(psA[:, half, :], ones128[:, :], hn_sq[:, 2 * half:2 * half + 2, :].rearrange("p a s -> p (a s)"),
                              start=True, stop=True).then_inc(sem(f"{tag}_mean"), 1)

            head_means("hg")
            pe.wait_ge(sem("hg_of"), 2)
            for n in range(4):
                x = (qT if n < 2 else kT)[:, 2 * (n % 2):2 * (n % 2) + 2, :].rearrange("p a s -> p (a s)")
                if n == 3:
                    pe.wait_ge(sem("rot1_done"), 1)
                pe.matmul(psW[:, n % 3, :], rotA, x, start=True, stop=True).then_inc(sem("rot1"), 1)

            pe.wait_ge(sem("rot1_done"), 4)
            pe.wait_ge(sem("hg_root"), 2)

            def scores(n):
                h, qt = n // 2, n % 2
                if n >= 2:
                    pe.wait_ge(sem("da_exp"), 2 * (n - 2) + 2)
                for m in range(2):
                    r = slice(64 * m, 64 * m + 64)
                    ins = pe.matmul(psX[:, 2 * (n % 2) + m, 0:256], qT[r, h, P * qt:P * qt + P], kT[r, h, :],
                                    start=True, stop=True, skip_group_check=True)
                ins.then_inc(sem("da_sc"), 1)

            scores(0)
            for n in range(8):
                h, qt = n // 2, n % 2
                if n < 7:
                    scores(n + 1)
                pe.wait_ge(sem("da_diag"), n + 1)
                if n >= 2:
                    pe.wait_ge(sem("da_wt"), n - 1)
                for kt in range(2):
                    for m in range(2):
                        ins = pe.matmul(psA[:, n % 2, P * kt:P * kt + P], da_p[n % 2][:, m, P * kt:P * kt + P],
                                        da_d[n % 2][:, m, :], start=(kt == 0 and m == 0), stop=(m == 1), skip_group_check=True)
                ins.then_inc(sem("da_pt"), 1)
                if qt == 1:
                    pe.wait_ge(sem("da_wt"), n + 1)
                    for kt in range(2):
                        ins = pe.matmul(psA[:, 2 + h // 2, 256 * (h % 2):256 * (h % 2) + 256], dvt[:, kt, P * h:P * h + P],
                                        da_w[h % 2][:, kt, :], start=(kt == 0 and h % 2 == 0), stop=(kt == 1), skip_group_check=True)
                    ins.then_inc(sem("da_oh"), 1)
            head_means("da")

            pe.wait_ge(sem("hg_olo"), 2)
            pe.wait_ge(sem("da_olo"), 2)
            for j in range(4):
                if j == 3:
                    pe.wait_ge(sem("x_ready"), 3)
                gemm(OUT1 + j, psW[:, j % 3, :], oh, ol)

            def down(b, i, f, first):
                have(b, i)
                pe.wait_ge(sem("flo_ready"), FSTEP * f + i + first)
                for o in range(KT):
                    for k in range(2):
                        ins = mm3(accv[:, o, :], (b, 2), lambda w: w[:, k, P * o:P * o + P], oh[:, k, :], ol[:, k, :], False, False)
                ins.then_inc(sem("wt_used"), 1)

            def ada_sums(g):
                pe.wait_ge(sem("ada_used"), 2 * g + 3)
                if not (isinstance(g, int) and g == 0):
                    pe.wait_ge(sem("mod_ready"), g + 1)
                for k in range(4):
                    ins = pe.matmul(psS[:, 256 + k:257 + k], adacc[:, P * k:P * k + P], ones[:, 0:1], start=True, stop=True,
                                    skip_group_check=True)
                ins.then_inc(sem("ada_sum"), 1)

            def ffn(b, f, norm_m, p, ada, acc_free):
                mean(norm_m)
                pe.wait_ge(sem(acc_free[0]), acc_free[1])
                pe.wait_ge(sem("small_set"), 1)
                for a in range(4):
                    pe.matmul(psA[:, a, :], zeros[:, :], zeros[:, 0:1].broadcast_to([P, 512]), start=True, stop=False, skip_group_check=True)
                gemm(b, psW[:, 0, :], hh, hl, first=p)
                gemm(b + 1, psW[:, 1, :], hh, hl)

                def step(bb, i, first, g):
                    if f == 0:
                        pe.wait_ge(sem("conv_ready"), FSTEP * f + i + first)
                    else:
                        pe.wait_ge(sem("ge_ready"), FSTEP * f + i + first)
                    gemm(bb, psW[:, 0, :], hh, hl, i)
                    pe.wait_ge(sem("actf_ready"), FSTEP * f + i + first)
                    gemm(bb + 1, psW[:, 1, :], hh, hl, i)
                    down(bb + 2, i, f, first)
                    if g is not None:
                        ada_sums(g + i)

                loops = [(9, 0)] if f != 1 else [(8, 0), (1, 8)]
                for cnt, i0 in loops:
                    bb = b + 2 + 3 * i0
                    g = None if ada is None else ada + i0
                    if cnt > 1:
                        with pe.Fori(0, cnt) as i:
                            step(bb, i, i0 + 1, g)
                    else:
                        step(bb, 0, i0 + 1, g)
                step(b + 29, 0, 10, None)
                down(b + 32, 0, f, 11)

            ffn(FFN1, 0, 1, 1, 0, ("da_of", 2))

            pe.wait_ge(sem("x_ready"), 8)
            have(PLE)
            for o in range(KT):
                for k in range(2):
                    ins = mm3(accv[:, o, :], (PLE, 2), lambda w: w[:, k, P * o:P * o + P], pTh[:, k, :], pTl[:, k, :],
                              o % 2 == 0 and k == 0, k == 1)
            ins.then_inc(sem("wt_used"), 1)
            mean(2)
            for j in range(4):
                if j == 3:
                    pe.wait_ge(sem("pg_sig"), 1)
                gemm(PGATE + j, psW[:, j % 3, :], hh, hl, first=2 if j == 0 else None)
            mean(3)
            ffn(FFN2, 1, 4, 3, 9, ("x_ready", 12))

            mean(5)

            def head_mean(n):
                w = 256 if IN2_COLS[n][0] == "misc" else 512
                pe.wait_ge(sem("m_sq"), n + 1)
                if n:
                    pe.wait_ge(sem("m_root"), n)
                pe.matmul(psS[:, 0:w], mean64, m_sq[:, 0:w], start=True, stop=True).then_inc(sem("m_mean"), 1)

            for j, (what, c0) in enumerate(IN2_COLS):
                b = IN2 + j
                bank = psW[:, j % 3, :]
                if j >= 3:
                    r = j - 3
                    if r <= 6:
                        pe.wait_ge(sem("in2_read_dve"), r + 1)
                        if r == 6:
                            pe.wait_ge(sem("misc_act"), 1)
                    elif r > 7:
                        pe.wait_ge(sem("in2_read_act"), r - 7)
                if what == "fv":
                    gemm_tok(b, bank)
                elif (what, c0) == ("misc", 1):
                    have(b)
                    for k in range(KT):
                        mm3(psA[:, 0, 0:S], (b, KT), lambda w: w[:, k, 8:136], hh[:, k, :], hl[:, k, :], k == 0, k == KT - 1)
                    for t in range(TT):
                        for k in range(KT):
                            mm3t(psA[:, 1, 8 * t:8 * t + 8], (b, KT), lambda w: w[:, k, 0:8],
                                 hh[:, k, P * t:P * t + P], hl[:, k, P * t:P * t + P], k == 0, k == KT - 1)
                        for k in range(KT):
                            ins = mm3t(psA[:, 1, P + 64 * t:P + 64 * t + 64], (b, KT), lambda w: w[:, k, 64:128],
                                       hh[:, k, P * t:P * t + P], hl[:, k, P * t:P * t + P], k == 0, k == KT - 1)
                    ins.then_inc(sem("wt_used"), 1)
                else:
                    gemm(b, bank, hh, hl, first=4 if j == 0 else None)
                if 1 <= j <= 7:
                    head_mean(j - 1)
            pe.wait_ge(sem("in2_read_dve"), 7)
            pe.wait_ge(sem("misc_act"), 3)
            pe.wait_ge(sem("in2_read_act"), 11)
            pe.wait_ge(sem("ff_x"), 1)
            for n in range(2):
                pe.matmul(psA[:, n, :], rotA, dqT[:, 2 * n:2 * n + 2, :].rearrange("p a s -> p (a s)"), start=True, stop=True)
            pe.matmul(psA[:, 2, :], rotI, iqT.rearrange("p a s -> p (a s)"), start=True, stop=True)
            pe.matmul(psA[:, 3, 0:S], rotA, dkT, start=True, stop=True, skip_group_check=True)
            pe.matmul(psA[:, 3, S:2 * S], rotI, ikT, start=True, stop=True, skip_group_check=True).then_inc(sem("rot2"), 1)
            pe.wait_ge(sem("rot2_done"), 1)
            pe.wait_ge(sem("F_ready"), 1)

            def softmax_heads(tag, score, v_of, prev):
                def sc(h):
                    if h >= 3:
                        pe.wait_ge(sem(f"{tag}_max"), 2 * (h - 3) + 2)
                    score(h, psW[:, h % 3, :]).then_inc(sem(f"{tag}_sc"), 1)

                if prev:
                    pe.wait_ge(sem(prev[0]), prev[1])
                sc(0)
                for h in range(8):
                    if h < 7:
                        sc(h + 1)
                    pe.wait_ge(sem(f"{tag}_diag"), h + 1)
                    if h >= 2:
                        pe.wait_ge(sem(f"{tag}_wt"), h - 1)
                    p, d = m_p[h % 2], m_d[h % 2]
                    bank = psA[:, h % 2, :]
                    pe.matmul(bank[:, 0:128], p[:, 0:128], d[:, 0, :], start=True, stop=True, skip_group_check=True)
                    pe.matmul(bank[:, 128:256], p[:, 128:256], d[:, 1, :], start=False, stop=True, skip_group_check=True)
                    pe.matmul(bank[:, 256:384], p[:, 256:384], d[:, 1, :], start=False, stop=True, skip_group_check=True).then_inc(sem(f"{tag}_pt"), 1)
                    pe.wait_ge(sem(f"{tag}_wt"), h + 1)
                    w = m_w[h % 2]
                    rows = slice(64 * (h % 2), 64 * (h % 2) + 64)
                    t = h // 2
                    dst = psA[rows, 2 + t // 2, 256 * (t % 2):256 * (t % 2) + 256]
                    pe.matmul(dst, v_of(h, 0), w[:, 0:256], start=(t % 2 == 0), stop=False, skip_group_check=True)
                    pe.matmul(dst[:, P:2 * P], v_of(h, 1), w[:, 256:384], start=False, stop=True,
                              skip_group_check=True).then_inc(sem(f"{tag}_pv"), 1)

            def fox_score(h, bank):
                r = slice(64 * (h % 2), 64 * (h % 2) + 64)
                for qt in range(2):
                    w = P * (qt + 1)
                    dst = bank[:, P * qt:P * qt + w]
                    q = slice(P * qt, P * qt + P)
                    pe.matmul(dst, fqT[r, h // 2, q], fkT[r, h // 2, 0:w], start=(qt == 0), stop=False, skip_group_check=True)
                    c = 64 * (h % 2) + h
                    pe.matmul(dst, Fc[r, q], ident[r, c:c + 1].broadcast_to([64, w]), start=False, stop=False, skip_group_check=True)
                    ins = pe.matmul(dst, negid[r, c:c + 1].broadcast_to([64, P]), Fc[r, 0:w], start=False, stop=True, skip_group_check=True)
                return ins

            pe.wait_ge(sem("setup_done"), 1)
            softmax_heads("fox", fox_score, lambda h, kt: fvt[:, kt, 64 * h:64 * h + 64], None)

            pe.wait_ge(sem("fox_wt"), 8)
            pe.wait_ge(sem("fox_olo"), 2)
            for qt in range(2):
                w = P * (qt + 1)
                if qt == 1:
                    pe.wait_ge(sem("ix_relu"), 1)
                for h in range(8):
                    t = h % 4
                    r = slice(32 * t, 32 * t + 32)
                    ins = pe.matmul(psA[:, t, (h // 4) * w:(h // 4) * w + w], iqT[r, h // 4, P * qt:P * qt + P], ikT[r, 0:w],
                                    start=(h < 4), stop=True, skip_group_check=True, tile_position=(32 * t, 0))
                ins.then_inc(sem("ix_dots"), 1)

            def dsa_score(h, bank):
                r = slice(64 * (h % 2), 64 * (h % 2) + 64)
                for qt in range(2):
                    w = P * (qt + 1)
                    ins = pe.matmul(bank[:, P * qt:P * qt + w], dqT[r, h // 2, P * qt:P * qt + P], dkT[r, 0:w],
                                    start=(qt == 0), stop=True, skip_group_check=True)
                return ins

            pe.wait_ge(sem("ix_relu"), 2)
            softmax_heads("dsa", dsa_score, lambda h, kt: dvt2[:, kt, :], ("fox_max", 16))

            pe.wait_ge(sem("fox_olo"), 2)
            pe.wait_ge(sem("dsa_olo"), 2)
            for j in range(4):
                b, c, br = BRANCH + j, j // 2, j % 2
                have(b)
                if c:
                    pe.wait_ge(sem("mg_lo"), 2)
                for o in range(4):
                    for k in range(4):
                        ins = mm3(psA[:, 2 * br + o // 2, 256 * (o % 2):256 * (o % 2) + 256], (b, 4),
                                  lambda w: w[:, k, P * o:P * o + P], oh[:, 4 * br + k, :], ol[:, 4 * br + k, :],
                                  k == 0 and o % 2 == 0, k == 3)
                ins.then_inc(sem("wt_used"), 1)
            pe.wait_ge(sem("mg_lo"), 4)
            for j in range(4):
                if j == 3:
                    pe.wait_ge(sem("x_ready"), 30)
                gemm(OUT2 + j, psW[:, j % 3, :], hh, hl)
            ffn(FFN3, 2, 6, 5, None, ("mg_lo", 4))
            pe.wait_ge(sem("x_ready"), 44)
            for t in range(TT):
                for k in range(KT):
                    ins = pe.transpose(psA[:, 2 * t + k // 4, P * (k % 4):P * (k % 4) + P],
                                       xT[:, k, P * t:P * t + P], ident)
                ins.then_inc(sem("out_tr"), 1)




_NAMES = ["x", "p", "positions", "norm_mix_g", "w_in", "lam_q1", "lam_k1", "lam_q2", "lam_k2", "da_subln_g",
          "hg_lb_gamma", "hg_norm_g", "w_out", "norm_ffn_g", "w_ffn_gate", "w_ffn_up", "ffn_conv_w", "ffn_conv_b",
          "w_ffn_down", "norm_ple_g", "w_ple", "w_ple_gate", "final_norm_g", "c_2", "positions_2", "ada_w_2",
          "ada_b_2", "norm_g_2", "ffn1_w1_2", "ffn1_w3_2", "ffn1_w2_2", "w_in_2", "fox_f_bias_2", "fox_qk_g_2",
          "dsa_qk_g_2", "w_br_fox_2", "w_br_dsa_2", "w_out_2", "ffn2_w1_2", "ffn2_w3_2", "ffn2_w2_2"]


def kernel(**inputs):
    import concourse.bacc as bacc
    from concourse.bass_utils import run_bass_kernel_spmd

    nc = bacc.Bacc("TRN2", target_bir_lowering=False, num_devices=1)
    arrays, args = {}, {}
    for name in _NAMES:
        a = np.ascontiguousarray(inputs[name])
        arrays[f"in_{name}"] = a
        args[name] = nc.dram_tensor(f"in_{name}", a.shape, mybir.dt.from_np(a.dtype), kind="ExternalInput").ap()
    arrays["in_consts"] = constants()
    args["consts"] = nc.dram_tensor("in_consts", (P, CONST_N), F32, kind="ExternalInput").ap()
    out = nc.dram_tensor("out_x", (1, S, D), F32, kind="ExternalOutput").ap()
    two_blocks(nc, args, out)
    r = run_bass_kernel_spmd(nc, [arrays], core_ids=[0])
    return r.results[0]["out_x"]
```

```python
from contextlib import ExitStack

import numpy as np

import concourse.bass as bass
from concourse import mybir

ALU = mybir.AluOpType
ACT = mybir.ActivationFunctionType
F32 = mybir.dt.float32
F32R = mybir.dt.float32r
I32 = mybir.dt.int32
BF16 = mybir.dt.bfloat16
AXX = mybir.AxisListType.X

P = 128
S = 256
TT = S // P
D = 1024
KT = D // P
FF = 2816
FSTEP = FF // 256
ADA_UNITS = FSTEP
ADA_TAIL = (9 * D - 256 * FSTEP - 512 * FSTEP) // 256
MOD_AT = [0, 2 * FSTEP, 6 * FSTEP, 9 * KT]
X_IN, X_OUT1, X_FFN1, X_PGATE, X_FINAL, X_FFN2, X_OUT2, X_END = 0, 2, 6, 14, 18, 26, 34, 50
EPS = 1e-6
BIG = -1e30
PICKED = -3e38
TOPK = S // 4
LAMBDA_INIT = 0.2
THETA = 500000.0

IN1, OUT1, FFN1, PLE, PGATE = 0, 16, 20, 53, 54
FFN2, IN2, BRANCH, OUT2, FFN3, CHUNKS = 58, 91, 110, 114, 118, 151
RING = 3

IN1_COLS = [("zf", 2048), ("zf", 2304), ("zb", 2560), ("zb", 2816), ("g", 3584), ("g", 3840),
            ("hq", 1536), ("hq", 1792), ("hv", 3072), ("hv", 3328), ("dq", 0), ("dq", 256),
            ("dk", 512), ("dk", 768), ("dv", 1024), ("dv", 1280)]
IN2_COLS = [("fq", 0), ("ga", 2480), ("fq", 256), ("ga", 2736), ("fk", 512), ("ga", 2992), ("fk", 768),
            ("ga", 3248), ("dq", 1544), ("fv", 1024), ("dq", 1800), ("fv", 1280), ("misc", 0), ("misc", 1),
            ("iq", 2184), ("gb", 3504), ("gb", 3760), ("gb", 4016), ("gb", 4272)]
GB = 15
NORM_AT = [j for j, (what, c) in enumerate(IN2_COLS) if what in ("fq", "fk", "dq") or (what, c) == ("misc", 0)]
MISC = [[(0, 2056, 64), (64, 2056, 64)] + [(128 + 32 * i, 2440, 32) for i in range(4)],
        [(0, 2472, 8), (8, 1536, 8), (64, 2120, 64)]]

LEVEL_AT = [10, 11, 12, 13, 14, 15]

ROWS_A = [("conv_w", 66), ("conv_b", 22), ("norm_mix", 8), ("norm_ffn", 8), ("norm_ple", 8),
          ("final", 8), ("subln", 1), ("hgnorm", 1)]
ROWS_B = [("ada_b", 72), ("norm_g", 24), ("c", 8), ("gamma", 16), ("foxg", 2), ("dsag", 2)]


def offsets(rows):
    at, out = 0, {}
    for name, n in rows:
        out[name] = at
        at += n
    return out, at


COL_A, NROW_A = offsets(ROWS_A)
COL_B, NROW_B = offsets(ROWS_B)

LEVELS = [128, 64, 32, 16, 8, 4, 2]
CONST = [("ident", 128), ("rotA", 128), ("rotI", 128), ("mean64", 128), ("causal", 256),
         ("admit", 256), ("levels", 128 * (len(LEVELS) - 1)), ("freq", 2)]
CONST_AT, CONST_N = offsets(CONST)


def constants():
    out = np.zeros((P, CONST_N), np.float32)
    p = np.arange(P)

    def part(name):
        at = CONST_AT[name]
        return out[:, at:at + dict(CONST)[name]]

    part("ident")[p, p] = 1.0
    for name, period, half in (("rotA", 64, 8), ("rotI", 32, 4)):
        for m in range(P):
            if m % period < half:
                part(name)[m + half, m] = -1.0
            elif m % period < 2 * half:
                part(name)[m - half, m] = 1.0
    part("mean64")[:, :] = (p[:, None] // 64 == p[None, :] // 64) / 64.0
    part("causal")[:, P:] = np.where(p[None, :] <= p[:, None], 0.0, BIG)
    part("admit")[:, P:] = np.where(p[None, :] // 64 <= p[:, None] // 64, 0.0, BIG)
    for n, b in enumerate(LEVELS[1:]):
        same = p[:, None] // b == p[None, :] // b
        halves = p[:, None] // (b // 2) != p[None, :] // (b // 2)
        part("levels")[:, n * P:(n + 1) * P] = same & halves
    f_a = np.float32(THETA) ** (-np.arange(8, dtype=np.float32) / np.float32(8))
    f_i = np.float32(THETA) ** (-np.arange(0, 8, 2, dtype=np.float32) / np.float32(8))
    for m in range(P):
        if m % 64 < 16:
            part("freq")[m, 0] = f_a[m % 8]
        if m % 32 < 8:
            part("freq")[m, 1] = f_i[m % 4]
    return out


def two_blocks(nc, A, out):
    with ExitStack() as ctx:
        def sb(name, shape, dt=F32):
            return ctx.enter_context(nc.sbuf_tensor(name, [P] + shape, dt))

        def ps(name, shape):
            return ctx.enter_context(nc.psum_tensor(name, [P] + shape, F32))

        sems = {}

        def sem(name):
            if name not in sems:
                sems[name] = ctx.enter_context(nc.semaphore(name))
            return sems[name]

        raw = [sb(f"raw{r}", [2048]) for r in range(RING)]
        whi = [sb(f"whi{r}", [2048], F32R) for r in range(RING)]
        wlo = [sb(f"wlo{r}", [2048], F32R) for r in range(RING)]
        adacc = sb("adacc", [512])
        xT = sb("xT", [KT, S])
        hh = sb("hh", [KT, S], F32R)
        hl = sb("hl", [KT, S], F32R)
        oh = sb("oh", [KT, S], F32R)
        ol = sb("ol", [KT, S], F32R)
        pTh = sb("pTh", [2, S], F32R)
        pTl = sb("pTl", [2, S], F32R)
        con = sb("con", [CONST_N])
        trig = sb("trig", [3, 2, S])
        colsA = sb("colsA", [NROW_A])
        colsB = sb("colsB", [NROW_B])
        modT = sb("modT", [72])
        gain2 = sb("gain2", [24])
        small = sb("small", [64])
        ones1k = sb("ones1k", [P])
        ones128 = sb("ones128", [P])
        ones = sb("ones", [P])
        rootv = sb("rootv", [S])
        rstd = sb("rstd", [S])
        nb = sb("nb", [KT, S])
        SCR = 14400
        zeros = sb("zeros", [P], BF16)
        negid = sb("negid", [P])
        scr = sb("scr", [SCR])

        def region(start=0):
            at = [start]

            def take(*shape):
                n = int(np.prod(shape))
                v = scr[:, at[0]:at[0] + n]
                at[0] += n
                assert at[0] <= SCR, at[0]
                if len(shape) == 2:
                    return v.rearrange("p (a b) -> p a b", b=shape[1])
                if len(shape) == 3:
                    return v.rearrange("p (a b c) -> p a b c", b=shape[1], c=shape[2])
                if len(shape) == 4:
                    return v.rearrange("p (a b c d) -> p a b c d", b=shape[1], c=shape[2], d=shape[3])
                return v
            return take

        psA = ps("psA", [4, 512])
        psX = ps("psX", [4, 512])
        psW = psX[:, 0:3, :]
        psS = psX[:, 3, :]
        accv = psA[:, :, :].rearrange("p a (b c) -> p (a b) c", b=2)

        def cst(name, n=None):
            at = CONST_AT[name]
            return con[:, at:at + (n or dict(CONST)[name])]

        ident = cst("ident")
        rotA, rotI, mean64 = cst("rotA"), cst("rotI"), cst("mean64")

        def colA(name, k=0, n=1):
            return colsA[:, COL_A[name] + k:COL_A[name] + k + n]

        def colB(name, k=0, n=1):
            return colsB[:, COL_B[name] + k:COL_B[name] + k + n]

        eps, zero, one, nlam = (small[:, i:i + 1] for i in range(4))
        eps2 = small[:, 5:6]
        halfpi = small[:, 4:5]
        omlb, lb = small[:, 8:16], small[:, 16:24]
        subg = small[:, 24:25]
        foxg_q, dsag_q = small[:, 25:26], small[:, 26:27]
        lamt = small[:, 28:32]
        condT = small[:, 32:40]
        ffb = small[0:8, 40:41]
        gex = small[:, 48:64]

        take = region()
        xtok = take(TT, D)
        ptok = take(TT, S)
        rowsA, rowsB = take(P), take(P)
        take = region((6 * 4 + 8 + 8) * S)
        posi = take(3, S)
        ang, kr, red = take(3, S), take(3, S), take(3, S)
        lamr = take(4, 64)
        lamp = take(2, 64)

        take = region()
        qT, kT = take(4, S), take(4, S)
        dvt, hvt = take(TT, 512), take(TT, 512)
        hqT, gT = take(4, S), take(4, S)
        lf = take(8, S)
        kin = nb
        E = take(8, TT, 129)
        qk = [take(2, 1024) for _ in range(2)]
        AT = lf.rearrange("p (t h) s -> p t h s", t=TT)
        at_qk = [q.rearrange("p a b -> p (a b)") for q in qk]
        da_p = [at_qk[0][:, 512 * i:512 * i + 512].rearrange("p (m k) -> p m k", m=2) for i in range(2)]
        da_w = [at_qk[0][:, 1024 + 512 * i:1536 + 512 * i].rearrange("p (k q) -> p k q", k=2)
                for i in range(2)]
        da_d = [at_qk[1][:, 256 * i:256 * i + 256].rearrange("p (m q) -> p m q", m=2) for i in range(2)]
        da_s = at_qk[1][:, 512:640]
        rot1 = adacc[:, :]
        hn_sq = at_qk[0].rearrange("p (h s) -> p h s", h=8)[:, 0:4]
        hn_rt = at_qk[0].rearrange("p (h s) -> p h s", h=8)[:, 4:8]
        hn_of = at_qk[1].rearrange("p (h s) -> p h s", h=8)[:, 0:4]

        take = region()
        f_t, f_g, f_a = take(2, S), take(2, S), take(2, S)
        f_s = take(2, 512)
        adar = [take(2048) for _ in range(2)]
        nb2 = take(KT, S)

        take = region()
        fqT, fkT, dqT = take(4, S), take(4, S), take(4, S)
        fvt = take(TT, 512)
        dkT, ikT, iqT = take(S), take(S), take(2, S)
        dvt2, iwt = take(TT, 64), take(TT, 8)
        gaS, gbS = take(KT, S), take(KT, S)
        Fc = take(S)
        m_sq, m_rt, m_xn = take(512), take(512), take(512)
        m_p = [take(384) for _ in range(2)]
        m_w = [take(384) for _ in range(2)]
        lgs = [m_w[0][:, 0:S], m_w[1][:, 0:S], m_p[0][:, 0:S]]
        m_d = [take(2, P) for _ in range(2)]
        m_s = take(160)
        sc0, sc1 = take(P), take(S)
        top8 = take(8)
        reluv = nb[:, :, :].rearrange("p a b -> p (a b)")
        mg = m_sq.rearrange("p (a s) -> p a s", a=2)

        block = ctx.enter_context(nc.Block())

        def chunk_src(w, c0, cols=256):
            return w.rearrange("(k p) n -> p k n", p=P)[:, :, c0:c0 + cols]

        def kview(buf, k):
            return buf[:, :].rearrange("p (k n) -> p k n", k=k)

        @block.sync
        def _(sp):
            def load(b, srcs, i=0):
                if b >= RING:
                    sp.wait_ge(sem("lo_ready"), b - 2 + 3 * i)
                for n, (dst, src) in enumerate(srcs):
                    sp.dma_start(dst, src).then_inc(sem(f"raw{b % 3}"), 16)

            def cols(b, w, c0):
                return [(kview(raw[b % 3], KT), chunk_src(w, c0))]

            def rows2(b, w, r0):
                rows = slice(r0, r0 + 256) if isinstance(r0, int) else bass.ds(r0, 256)
                return [(kview(raw[b % 3], 2), w[rows, :].rearrange("(k p) n -> p k n", p=P))]

            def coldyn(b, w, c0):
                if isinstance(c0, int):
                    return cols(b, w, c0)
                return [(kview(raw[b % 3], KT), w.rearrange("(k p) n -> p k n", p=P)[:, :, bass.ds(c0, 256)])]

            small_load = sem("small_loaded")
            sp.dma_start(xtok, A["x"][0].rearrange("(t p) d -> p t d", p=P)).then_inc(sem("x_loaded"), 16)
            sp.dma_start(con[:, :], A["consts"]).then_inc(sem("con_loaded"), 16)
            rows = {
                "conv_w": A["ffn_conv_w"][0].rearrange("j (k p) -> (j k) p", p=P),
                "conv_b": A["ffn_conv_b"][0].rearrange("(k p) -> k p", p=P),
                "norm_mix": A["norm_mix_g"][0].rearrange("(k p) -> k p", p=P),
                "norm_ffn": A["norm_ffn_g"][0].rearrange("(k p) -> k p", p=P),
                "norm_ple": A["norm_ple_g"][0].rearrange("(k p) -> k p", p=P),
                "final": A["final_norm_g"].rearrange("(k p) -> k p", p=P),
                "subln": A["da_subln_g"], "hgnorm": A["hg_norm_g"],
                "ada_b": A["ada_b_2"][0].rearrange("(k p) -> k p", p=P),
                "norm_g": A["norm_g_2"][0].rearrange("j (k p) -> (j k) p", p=P),
                "c": A["c_2"][0].rearrange("(k p) -> k p", p=P),
                "gamma": A["hg_lb_gamma"].rearrange("z l (h p) -> (z l h) p", p=P),
            }
            for table, at, dst in ((ROWS_A, COL_A, rowsA), (ROWS_B, COL_B, rowsB)):
                for name, cnt in table:
                    if name in rows:
                        sp.dma_start(dst[at[name]:at[name] + cnt, :], rows[name]).then_inc(small_load, 16)
            for name, key in (("foxg", "fox_qk_g_2"), ("dsag", "dsa_qk_g_2")):
                a = COL_B[name]
                for half in range(2):
                    sp.dma_start(rowsB[a:a + 2, 64 * half:64 * half + 64], A[key][0]).then_inc(small_load, 16)
            load(0, cols(0, A["w_in"][0], IN1_COLS[0][1]))
            sp.dma_start(posi[:, 0, :].bitcast(I32), A["positions"][0].partition_broadcast(P)).then_inc(sem("pos_loaded"), 16)
            for j in (1, 2):
                sp.dma_start(posi[:, j, :].bitcast(I32), A["positions_2"][0].partition_broadcast(P)).then_inc(sem("pos_loaded"), 16)
            for j, name in enumerate(("lam_q1", "lam_k1", "lam_q2", "lam_k2")):
                sp.dma_start(lamr[:, j, :], A[name][0].partition_broadcast(P)).then_inc(sem("pos_loaded"), 16)
            sp.dma_start(ffb, A["fox_f_bias_2"].rearrange("a h -> h a")).then_inc(sem("pos_loaded"), 16)
            load(1, cols(1, A["w_in"][0], IN1_COLS[1][1]))
            sp.dma_start(ptok, A["p"][0, 0].rearrange("(t p) d -> p t d", p=P)).then_inc(sem("p_loaded"), 16)
            for j in range(2, 16):
                load(j, cols(j, A["w_in"][0], IN1_COLS[j][1]))
            for j in range(4):
                load(OUT1 + j, cols(OUT1 + j, A["w_out"][0], 256 * j))

            adaw = A["ada_w_2"][0].rearrange("(k p) n -> p k n", p=P)

            def ada(u, tile, r=0, cols=256, k0=0, ks=KT):
                if not (isinstance(u, int) and u == 0):
                    sp.wait_ge(sem(f"ada{r}_used"), u)
                c0 = P * tile
                c = slice(c0, c0 + cols) if isinstance(c0, int) else bass.ds(c0, cols)
                sp.dma_start(kview(adar[r], ks), adaw[:, k0:k0 + ks, c]).then_inc(sem(f"ada{r}_loaded"), 16)

            def ada_unit(u):
                ada(u, 2 * u)

            def ada_group(g, r):
                ada(g if r else g + ADA_UNITS, MOD_AT[1] + 4 * g, r, 512, 4 * r, 4)

            def ada_tail(v):
                ada(2 * FSTEP + v, MOD_AT[2] + 2 * v)

            def ffn(b, w1, w3, w2, piece, peel):
                load(b, cols(b, w1, 0))
                load(b + 1, cols(b + 1, w3, 0))
                if peel > 1:
                    sp.wait_ge(sem("x_ready"), X_OUT2 + 1)
                    piece(0, 2)

                def step(i, more=True):
                    for n, chunk in enumerate((coldyn(b + 2, w1, 256 * i + 256), coldyn(b + 3, w3, 256 * i + 256),
                                               rows2(b + 4, w2, 256 * i))):
                        load(b + 2 + n, chunk, i)
                        if more:
                            piece(i, n)

                step(0, False)
                for i in range(1, peel):
                    step(i)
                with sp.Fori(peel, FSTEP - 2) as i:
                    step(i, peel == 1)
                step(FSTEP - 2, peel == 1)
                load(b + 32, rows2(b + 32, w2, 256 * (FSTEP - 1)))

            def unit(i, n):
                if n == 2:
                    ada_unit(i)

            def group(i, n):
                if n:
                    ada_group(i, n - 1)

            def tail(i, n):
                if n == 2:
                    ada_tail(i)

            sp.wait_ge(sem("x_ready"), X_OUT1 + 1)
            ada_unit(0)
            ffn(FFN1, A["w_ffn_gate"][0], A["w_ffn_up"][0], A["w_ffn_down"][0], unit, 1)
            load(PLE, [(kview(raw[PLE % 3], 2), A["w_ple"][0].rearrange("(k p) n -> p k n", p=P))])
            for j in range(4):
                load(PGATE + j, cols(PGATE + j, A["w_ple_gate"][0], 256 * j))
                if j == 0:
                    ada_unit(FSTEP - 1)
            ada_group(0, 0)
            ada_group(0, 1)
            ffn(FFN2, *(A[f"ffn1_{w}_2"][0] for w in ("w1", "w3", "w2")), group, 1)
            wi = A["w_in_2"][0]
            for j, (what, c0) in enumerate(IN2_COLS):
                n = IN2 + j
                if what == "misc":
                    load(n, [(kview(raw[n % 3], KT)[:, :, at:at + w], chunk_src(wi, c, w)) for at, c, w in MISC[c0]])
                else:
                    load(n, cols(n, wi, c0))
                if j < 2:
                    ada_group(FSTEP - 1, j)
            for j in range(4):
                w = A["w_br_fox_2" if j % 2 == 0 else "w_br_dsa_2"][0]
                load(BRANCH + j, [(kview(raw[(BRANCH + j) % 3], 4), chunk_src(w, 512 * (j // 2), 512))])
            for j in range(4):
                load(OUT2 + j, cols(OUT2 + j, A["w_out_2"][0], 256 * j))
            ffn(FFN3, *(A[f"ffn2_{w}_2"][0] for w in ("w1", "w3", "w2")), tail, ADA_TAIL)
            o_v = out[0].rearrange("(t p) d -> p t d", p=P)
            for t in range(TT):
                sp.wait_ge(sem("out_ready"), t + 1)
                sp.dma_start(o_v[:, t, :], xtok[:, t, :]).then_inc(sem("stored"), 16)
            sp.wait_ge(sem("stored"), 32)

        def raw_count(b, i=0):
            extra = sum(len(MISC[m]) - 1 for m in range(2)
                        if b >= IN2 + NORM_AT[-1] + m and (b - IN2 - NORM_AT[-1] - m) % 3 == 0)
            return 16 * (b // 3 + 1 + extra) + 16 * i

        @block.scalar
        def _(act):
            a_ = nc.scalar

            def hi(b, i=0):
                if isinstance(i, int) and b + 3 * i >= CHUNKS:
                    return
                act.wait_ge(sem(f"raw{b % 3}"), raw_count(b, i))
                if b >= RING:
                    act.wait_ge(sem("wt_used"), b - 2 + 3 * i)
                a_.copy(whi[b % 3][:, :], raw[b % 3][:, :]).then_inc(sem("hi_ready"), 1)

            def norm(m, need, shift, meanwhile=None):
                for k in range(KT):
                    act.wait_ge(sem("x_ready"), need(k))
                    a_.activation(nb[:, k, :], xT[:, k, :], ACT.Square).then_inc(sem("sq_ready"), 1)
                    if m == 3:
                        a_.activation(nb2[:, k, :], xT[:, k, :], ACT.Square, scale=colA("final", k)).then_inc(sem("sq2_ready"), 1)
                if meanwhile:
                    meanwhile()
                act.wait_ge(sem("mean_ready"), m + 1)
                a_.activation(rootv[:, :], psS[:, 0:S], ACT.Sqrt, bias=eps).then_inc(sem("root_ready"), 1)
                if m == 3:
                    act.wait_ge(sem("both_ready"), 1)
                    a_.activation(f_t[:, 0, :], f_t[:, 0, :], ACT.Sqrt, bias=eps2).then_inc(sem("root2_ready"), 1)
                for k in range(KT):
                    act.wait_ge(sem("hs_ready"), KT * m + k + 1)
                    a_.activation(hh[:, k, :], nb[:, k, :], ACT.Identity,
                                  bias=shift(k)).then_inc(sem("hhi_ready"), 1)

            def level_exp(n):
                act.wait_ge(sem("lev_diff"), n + 1)
                a_.activation(qk[n % 2], qk[n % 2], ACT.Exp).then_inc(sem("lev_exp"), 1)

            act.wait_ge(sem("x_tr"), 1)
            act.wait_ge(sem("small_set"), 1)
            a_.copy(xT[:, 4:8, :], accv[:, 4:8, :]).then_inc(sem("x_copy"), 1)
            act.wait_ge(sem("gam_ready"), 1)
            a_.activation(gex, gex, ACT.Exp).then_inc(sem("gam_exp"), 1)
            a_.activation(condT, colB("c", 0, 8), ACT.Silu).then_inc(sem("cond_ready"), 1)
            norm(0, lambda k: 2, lambda k: zero, lambda: (hi(0), hi(1)))
            act.wait_ge(sem("p_tr"), 1)
            a_.copy(pTh[:, :, :], psW[:, 2, :].rearrange("p (k s) -> p k s", k=2)).then_inc(sem("p_hi"), 1)

            def log_f(heads):
                act.wait_ge(sem("in1_read_act"), 4)
                act.wait_ge(sem("sg_ready"), 4)
                act.wait_ge(sem("lb_ready"), 1)
                for d in heads:
                    a_.activation(lf[:, d, :], lf[:, d, :], ACT.Ln, bias=lb[:, d:d + 1],
                                  scale=omlb[:, d:d + 1]).then_inc(sem("lf_ready"), 1)

            for j, (what, c0) in enumerate(IN1_COLS):
                hi(IN1 + j + 2)
                bank = psW[:, j % 3, :]
                half = (j % 2) * 2
                two = bank.rearrange("p (a s) -> p a s", a=2)
                if j in LEVEL_AT:
                    level_exp(LEVEL_AT.index(j))
                act.wait_ge(sem("wt_used"), IN1 + j + 1)
                if what in ("zf", "zb"):
                    d = (4 if what == "zb" else 0) + half
                    a_.activation(lf[:, d:d + 2, :], two, ACT.Sigmoid).then_inc(sem("sg_ready"), 1)
                    a_.activation(kin[:, d:d + 2, :], two, ACT.Sigmoid, scale=-1.0).then_inc(sem("in1_read_act"), 1)
                elif what == "g":
                    a_.activation(gT[:, half:half + 2, :], two, ACT.Sigmoid).then_inc(sem("gsig_ready"), 1)
                elif what == "hv":
                    a_.copy(hvt[:, :, (j % 2) * 256:(j % 2) * 256 + 256], two).then_inc(sem("in1_read_act"), 1)
                elif what in ("dq", "dk"):
                    a_.copy((qT if what == "dq" else kT)[:, half:half + 2, :], two).then_inc(sem("in1_read_act"), 1)
                elif what == "dv":
                    a_.copy(dvt[:, :, (j % 2) * 256:(j % 2) * 256 + 256], two).then_inc(sem("in1_read_act"), 1)
                if j == 5:
                    act.wait_ge(sem("reduced"), 1)
                    a_.activation(trig[:, :, 1, :], red, ACT.Sin).then_inc(sem("act_set"), 1)
                    a_.activation(kr, red, ACT.Abs).then_inc(sem("act_set"), 1)
                    act.wait_ge(sem("act_set"), 2)
                    a_.activation(trig[:, :, 0, :], kr, ACT.Sin, bias=halfpi, scale=-1.0).then_inc(sem("act_set"), 1)
                if j == 6:
                    log_f(range(4))
                if j == 7:
                    log_f(range(4, 8))
                    act.wait_ge(sem("lam_ready"), 2)
                    a_.activation(lamt[:, 2:4], lamt[:, 0:2], ACT.Exp).then_inc(sem("lam_exp"), 1)

            for n in range(len(LEVEL_AT), len(LEVELS) + 1):
                level_exp(n)
            def head_norm(tag, src, step, o_ready, per_half):
                for half in range(2):
                    act.wait_ge(sem(o_ready), per_half * (half + 1))
                    a_.activation(hn_sq[:, 2 * half:2 * half + 2, :], src(half), ACT.Square).then_inc(sem(f"{tag}_sq"), 1)
                for half in range(2):
                    act.wait_ge(sem(f"{tag}_mean"), half + 1)
                    a_.activation(hn_rt[:, 2 * half:2 * half + 2, :], psA[:, half, :].rearrange("p (a s) -> p a s", a=2),
                                  ACT.Sqrt, bias=eps).then_inc(sem(f"{tag}_root"), 1)
                for half in range(2):
                    act.wait_ge(sem(f"{tag}_of"), half + 1)
                    at = step + 2 * half
                    a_.copy(oh[:, at:at + 2, :], hn_of[:, 2 * half:2 * half + 2, :]).then_inc(sem(f"{tag}_ohi"), 1)

            head_norm("hg", lambda h: psA[:, 2 + h, :].rearrange("p (a s) -> p a s", a=2), 4, "hg_o", 1)

            hi(OUT1 + 2)

            for n in range(8):
                h, qt = n // 2, n % 2
                act.wait_ge(sem("da_max"), n + 1)
                if n >= 2:
                    act.wait_ge(sem("da_pt"), n - 1)
                for m in range(2):
                    a_.activation(da_p[n % 2][:, m, :], psX[:, 2 * (n % 2) + m, 0:256], ACT.Exp,
                                  bias=da_s[:, 16 + 2 * n + m:17 + 2 * n + m], scale=0.125,
                                  accum_out=da_s[:, 32 + 2 * n + m:33 + 2 * n + m]).then_inc(sem("da_exp"), 1)
                act.wait_ge(sem("da_pt"), n + 1)
                if h >= 2:
                    act.wait_ge(sem("da_oh"), h - 1)
                a_.copy(da_w[h % 2][:, :, P * qt:P * qt + P],
                        psA[:, n % 2, 0:256].rearrange("p (k q) -> p k q", k=2)).then_inc(sem("da_wt"), 1)
            head_norm("da", lambda h: psA[:, 2 + h, :].rearrange("p (a s) -> p a s", a=2), 0, "da_oh", 2)
            for j in range(1, 4):
                hi(OUT1 + j + 2)

            def ffn(b, f):
                def gate(i):
                    if f == 0:
                        act.wait_ge(sem("conv_ready"), i + 1)
                    else:
                        act.wait_ge(sem("wt_used"), b + 3 * i + (1 if isinstance(i, int) and i == 0 else 0))
                    a_.activation(f_g, f_t if f == 0 else psW[:, 0, :].rearrange("p (a s) -> p a s", a=2),
                                  ACT.Gelu if f == 0 else ACT.Silu).then_inc(sem("ge_ready"), 1)

                def hidden_hi(i, q=0):
                    act.wait_ge(sem("actf_ready"), FSTEP * f + i + 1)
                    a_.copy(oh[:, q:q + 2, :], f_a).then_inc(sem("fhi_ready"), 1)

                def step(i):
                    hi(b + 5, i)
                    act.wait_ge(sem("actf_ready"), FSTEP * f + i + 1)
                    gate(i + 1)
                    if isinstance(i, int):
                        hidden_hi(i + 1, 2)
                        hi(b + 6, i)
                        hi(b + 7, i)
                        return
                    hi(b + 6, i)
                    hi(b + 7, i)
                    act.wait_ge(sem("wt_used"), b + 5 + 3 * i)
                    hidden_hi(i + 1)

                hi(b + 2)
                if f:
                    act.wait_ge(sem("actf_ready"), FSTEP * f)
                gate(0)
                hi(b + 3)
                hi(b + 4)
                hidden_hi(0)
                with act.Fori(0, FSTEP - 2) as i:
                    step(i)
                step(FSTEP - 2)

            norm(1, lambda k: X_OUT1 + k // 2 + 1, lambda k: zero)
            a_.preload_act_table(ACT.Gelu)
            ffn(FFN1, 0)
            norm(2, lambda k: X_FFN1 + k + 1, lambda k: zero)
            hi(PLE + 2)
            for j in range(4):
                hi(PGATE + j + 2)
                act.wait_ge(sem("wt_used"), PGATE + j + 1)
                if j >= 2:
                    act.wait_ge(sem("x_ready"), X_PGATE + j - 1)
                a_.activation(f_s[:, j % 2, :], psW[:, j % 3, :], ACT.Sigmoid).then_inc(sem("pg_sig"), 1)
            norm(3, lambda k: X_PGATE + k // 2 + 1, lambda k: modT[:, k:k + 1])
            a_.preload_act_table(ACT.Silu)
            ffn(FFN2, 1)
            norm(4, lambda k: X_FFN2 + k + 1, lambda k: modT[:, 24 + k:25 + k])

            def head_rms(n, width, post=None):
                act.wait_ge(sem("m_mean"), n + 1)
                if n:
                    act.wait_ge(sem("in2_read_dve"), n)
                a_.activation(m_rt[:, 0:width], psS[:, 0:width], ACT.Sqrt, bias=eps).then_inc(sem("m_root"), 1)

            for j, (what, c0) in enumerate(IN2_COLS[:GB]):
                hi(IN2 + j + 2)
                if j - 1 in NORM_AT:
                    head_rms(NORM_AT.index(j - 1), 256 if IN2_COLS[j - 1][0] == "misc" else 512)
                if j == GB - 1:
                    act.wait_ge(sem("ff_x"), 1)
                    a_.activation(lgs[1][0:8, :], lgs[0][0:8, :], ACT.Abs).then_inc(sem("ff_act"), 1)
                    act.wait_ge(sem("ff_act"), 1)
                    a_.activation(lgs[1][0:8, :], lgs[1][0:8, :], ACT.Exp, scale=-1.0).then_inc(sem("ff_act"), 1)
                    act.wait_ge(sem("ff_act"), 2)
                    a_.activation(lgs[1][0:8, :], lgs[1][0:8, :], ACT.Ln, bias=one[0:8, :]).then_inc(sem("ff_act"), 1)
                act.wait_ge(sem("wt_used"), IN2 + j + 1)
                bank = psW[:, j % 3, :]
                two = bank.rearrange("p (a s) -> p a s", a=2)
                if what in ("fq", "fk", "dq") or (what, c0) == ("misc", 0):
                    w = 256 if what == "misc" else 512
                    if j >= 1:
                        act.wait_ge(sem("m_mean"), NORM_AT.index(j))
                    a_.activation(m_sq[:, 0:w], bank[:, 0:w], ACT.Square).then_inc(sem("m_sq"), 1)
                    if what == "misc":
                        a_.copy(ikT, bank[:, 256:512]).then_inc(sem("misc_act"), 1)
                elif what == "misc":
                        a_.copy(iwt, psA[:, 1, 0:16].rearrange("p (t c) -> p t c", t=2)).then_inc(sem("misc_act"), 1)
                        a_.copy(dvt2, psA[:, 1, 128:256].rearrange("p (t c) -> p t c", t=2)).then_inc(sem("misc_act"), 1)
                elif what == "iq":
                    a_.copy(iqT, two).then_inc(sem("in2_read_act"), 1)
                elif what == "fv":
                    a_.copy(fvt[:, :, c0 - 1024:c0 - 768], two).then_inc(sem("in2_read_act"), 1)
                elif what == "ga":
                    k = j - 1
                    a_.activation(gaS[:, k:k + 2, :], two, ACT.Sigmoid).then_inc(sem("in2_read_act"), 1)
            def softmax_heads(tag, base):
                for h in range(8):
                    for qt in range(2):
                        act.wait_ge(sem(f"{tag}_max"), 2 * h + qt + 1)
                        if h >= 2:
                            act.wait_ge(sem(f"{tag}_pt"), h - 1)
                        v = m_p[h % 2][:, 0:128] if qt == 0 else m_p[h % 2][:, 128:384]
                        c = 2 * h + qt
                        a_.activation(v, v, ACT.Exp, bias=m_s[:, 32 + c:33 + c], scale=1.0,
                                      accum_out=m_s[:, 64 + c:65 + c]).then_inc(sem(f"{tag}_exp"), 1)
                    act.wait_ge(sem(f"{tag}_pt"), h + 1)
                    if h >= 2:
                        act.wait_ge(sem(f"{tag}_pv"), h - 1)
                    a_.copy(m_w[h % 2], psA[:, h % 2, 0:384]).then_inc(sem(f"{tag}_wt"), 1)
                for c in range(2):
                    act.wait_ge(sem(f"{tag}_pv"), 4 * c + 4)
                    dst = slice(4 * base + 2 * c, 4 * base + 2 * c + 2)
                    a_.copy(oh[:, dst, :], psA[:, 2 + c, :].rearrange("p (a s) -> p a s", a=2)).then_inc(sem(f"{tag}_ohi"), 1)

            softmax_heads("fox", 0)
            scale_i = 32 ** -0.5
            for qt in range(2):
                act.wait_ge(sem("ix_dots"), qt + 1)
                if qt == 1:
                    act.wait_ge(sem("ix_sum"), 1)
                w = 2 * P * (qt + 1)
                a_.activation(reluv[:, 0:4 * w].rearrange("p (a b) -> p a b", a=4), psA[:, :, 0:w], ACT.Relu,
                              scale=scale_i).then_inc(sem("ix_relu"), 1)
            for c in range(4):
                hi(IN2 + GB + c + 2)
                act.wait_ge(sem("wt_used"), IN2 + GB + c + 1)
                a_.copy(gbS[:, 2 * c:2 * c + 2, :], psX[:, c, :].rearrange("p (a s) -> p a s", a=2)).then_inc(sem("gb_read"), 1)
            softmax_heads("dsa", 1)
            act.wait_ge(sem("gb_read"), 4)
            for c in range(2):
                a_.activation(gbS[:, 4 * c:4 * c + 4, :], gbS[:, 4 * c:4 * c + 4, :], ACT.Sigmoid).then_inc(sem("gb_ready"), 1)

            for c in range(2):
                hi(BRANCH + 2 * c + 2)
                hi(BRANCH + 2 * c + 3)
                for t in range(2):
                    act.wait_ge(sem("mg_ready"), 2 * c + t + 1)
                    k = 4 * c + 2 * t
                    a_.copy(hh[:, k:k + 2, :], mg).then_inc(sem("mg_hi"), 1)
            for j in range(4):
                hi(OUT2 + j + 2)
            norm(5, lambda k: X_OUT2 + k + 1, lambda k: modT[:, 48 + k:49 + k])
            a_.preload_act_table(ACT.Silu)
            ffn(FFN3, 2)
            act.wait_ge(sem("out_tr"), 1)
            a_.copy(xtok[:, 0, :], psA[:, 0:2, :].rearrange("p a b -> p (a b)")).then_inc(sem("out_ready"), 1)
            act.wait_ge(sem("out_tr"), 2)
            a_.copy(xtok[:, 1, :], psA[:, 2:4, :].rearrange("p a b -> p (a b)")).then_inc(sem("out_ready"), 1)

        @block.vector
        def _(dve):
            v_ = nc.vector
            chain = [0, 0, 0]

            def link(ins):
                chain[0] += 1
                ins.then_inc(sem("dve_link"), 1)
                dve.wait_ge(sem("dve_link"), chain[0] + chain[1] * chain[2])

            def lo(b, i=0):
                if isinstance(i, int) and b + 3 * i >= CHUNKS:
                    return
                dve.wait_ge(sem("hi_ready"), b + 1 + 3 * i)
                v_.tensor_tensor(wlo[b % 3][:, :], raw[b % 3][:, :], whi[b % 3][:, :].bitcast(F32),
                                 ALU.subtract).then_inc(sem("lo_ready"), 1)

            def modulation(pieces, c0, c1):
                dve.wait_ge(sem("ada_sum"), pieces)
                link(v_.tensor_tensor(modT[:, c0:c1], psS[:, 256 + c0:256 + c1], colB("ada_b", c0, c1 - c0), ALU.add))

            def gains(s):
                link(v_.scalar_tensor_tensor(gain2[:, 8 * s:8 * s + 8], modT[:, 24 * s + 8:24 * s + 16], 1.0,
                                             colB("norm_g", 8 * s, 8), ALU.add, ALU.mult))

            def norm(m, gain, shift):
                dve.wait_ge(sem("root_ready"), m + 1)
                if m == 3:
                    v_.tensor_copy(f_g[:, 0, :], psS[:, 0:S]).then_inc(sem("mean_copy"), 1)
                    dve.wait_ge(sem("mean_copy"), 1)
                    dve.wait_ge(sem("mean2_ready"), 1)
                    v_.scalar_tensor_tensor(f_t[:, 0, :], f_g[:, 0, :], eps, psW[:, 1, 0:S],
                                            ALU.mult, ALU.add).then_inc(sem("both_ready"), 1)
                    modulation(FSTEP, MOD_AT[0], MOD_AT[1])
                    gains(0)
                    link(v_.tensor_tensor(f_s[:, 0, 0:8], gain2[:, 0:8], colA("final", 0, 8), ALU.mult))
                    dve.wait_ge(sem("root2_ready"), 1)
                    link(v_.reciprocal(rstd[:, :], f_t[:, 0, :]))
                else:
                    link(v_.reciprocal(rstd[:, :], rootv[:, :]))

                def low(k):
                    dve.wait_ge(sem("hhi_ready"), KT * m + k + 1)
                    v_.scalar_tensor_tensor(hl[:, k, :], nb[:, k, :], shift(k), hh[:, k, :].bitcast(F32),
                                            ALU.add, ALU.subtract).then_inc(sem("hlo_ready"), 1)

                for k in range(KT):
                    v_.scalar_tensor_tensor(nb[:, k, :], xT[:, k, :], gain(k), rstd[:, :],
                                            ALU.mult, ALU.mult).then_inc(sem("hs_ready"), 1)
                    if k:
                        low(k - 1)
                low(KT - 1)

            v_.memset(ones1k[:, :], 1.0 / D)
            v_.memset(ones128[:, :], 1.0 / P)
            v_.memset(ones[:, :], 1.0)
            v_.memset(zero, 0.0)
            v_.memset(zeros[:, :], 0.0)
            v_.memset(one, 1.0)
            v_.memset(eps2, EPS * EPS)
            v_.memset(halfpi, float(np.pi / 2))
            v_.memset(eps, EPS).then_inc(sem("small_set"), 1)
            dve.wait_ge(sem("cols_tr"), 1)
            v_.tensor_copy(colsA[:, :], psS[:, 0:NROW_A])
            v_.tensor_copy(colsB[:, :], psS[:, P:P + NROW_B]).then_inc(sem("cols_ready"), 1)
            v_.tensor_copy(xT[:, 0:4, :], accv[:, 0:4, :]).then_inc(sem("x_ready"), 1)
            dve.wait_ge(sem("x_copy"), 1)
            dve.wait_ge(sem("cols_ready"), 1)
            v_.tensor_scalar(subg, colA("subln"), 1.0 - LAMBDA_INIT, None, ALU.mult).then_inc(sem("x_ready"), 1)
            gm = colB("gamma", 0, 16).rearrange("p (z l h) -> p z l h", z=2, l=2)
            ge = gex.rearrange("p (z l h) -> p z l h", z=2, l=2)
            mx = small[:, 8:16].rearrange("p (z h) -> p z h", z=2)
            link(v_.tensor_tensor(mx, gm[:, :, 0, :], gm[:, :, 1, :], ALU.max))
            v_.tensor_tensor(ge[:, :, 0, :], gm[:, :, 0, :], mx, ALU.subtract)
            v_.tensor_tensor(ge[:, :, 1, :], gm[:, :, 1, :], mx, ALU.subtract).then_inc(sem("gam_ready"), 1)
            v_.tensor_scalar(foxg_q, colB("foxg"), 0.125, None, ALU.mult)
            v_.tensor_scalar(dsag_q, colB("dsag"), 0.125, None, ALU.mult)
            dve.wait_ge(sem("gam_exp"), 1)
            link(v_.tensor_tensor(mx, ge[:, :, 0, :], ge[:, :, 1, :], ALU.add))
            link(v_.reciprocal(mx, mx))
            lbv = lb.rearrange("p (z h) -> p z h", z=2)
            link(v_.tensor_tensor(lbv, ge[:, :, 0, :], mx, ALU.mult))
            v_.tensor_scalar(omlb, lb, -1.0, 1.0, ALU.mult, ALU.add).then_inc(sem("lb_ready"), 1)
            lo(0)
            lo(1)
            norm(0, lambda k: colA("norm_mix", k), lambda k: zero)
            dve.wait_ge(sem("p_hi"), 1)
            v_.tensor_tensor(pTl[:, :, :], psW[:, 2, :].rearrange("p (k s) -> p k s", k=2), pTh[:, :, :].bitcast(F32),
                             ALU.subtract).then_inc(sem("p_lo"), 1)

            def angles(part):
                magic = 12582912.0
                c1 = 6.28125
                c2 = float(np.float32(int((2 * np.pi - c1) * 2 ** 18) / 2 ** 18))
                c3 = float(np.float32(2 * np.pi - c1 - c2))
                if part == 0:
                    dve.wait_ge(sem("pos_loaded"), 128)
                    dve.wait_ge(sem("con_loaded"), 16)
                    freq = cst("freq")
                    v_.tensor_scalar(negid[:, :], ident, -1.0, None, ALU.mult)
                    link(v_.tensor_copy(ang, posi.bitcast(I32)))
                    v_.tensor_scalar(ang[:, 0:2, :], ang[:, 0:2, :], freq[:, 0:1], None, ALU.mult)
                    link(v_.tensor_scalar(ang[:, 2, :], ang[:, 2, :], freq[:, 1:2], None, ALU.mult))
                elif part == 1:
                    link(v_.tensor_scalar(kr, ang, float(1 / (2 * np.pi)), magic, ALU.mult, ALU.add))
                    link(v_.tensor_scalar(kr, kr, -magic, None, ALU.add))
                elif part == 2:
                    link(v_.scalar_tensor_tensor(red, kr, -c1, ang, ALU.mult, ALU.add))
                    link(v_.scalar_tensor_tensor(red, kr, -c2, red, ALU.mult, ALU.add))
                else:
                    link(v_.scalar_tensor_tensor(red, kr, -c3, red, ALU.mult, ALU.add))
                    v_.tensor_scalar(red, red, 3.1415925, -3.1415925, ALU.min, ALU.max).then_inc(sem("reduced"), 1)

            Ef, Eb = E[:, 0:4], E[:, 4:8]
            qh = hqT.rearrange("p h (t s) -> p h t s", t=2)
            kf = kin[:, 0:4].rearrange("p h (t s) -> p h t s", t=2)
            kb = kin[:, 4:8].rearrange("p h (t s) -> p h t s", t=2)

            def qk_of(n):
                q, k = qk[n % 2][:, 0, :], qk[n % 2][:, 1, :]
                return (x.rearrange("p (h t s) -> p h t s", h=4, t=2) for x in (q, k))

            def diffs(n):
                if n >= 2:
                    dve.wait_ge(sem("lev_mm"), n - 1)
                if n == 0:
                    Q, K = qk_of(n)
                    tot_b = Eb[:, :, 0, 128:129].broadcast_to([P, 4, P])
                    tot_f = Ef[:, :, 0, 128:129].broadcast_to([P, 4, P])
                    v_.tensor_copy(Q[:, :, 1, :], Ef[:, :, 1, 1:129])
                    v_.tensor_tensor(Q[:, :, 0, :], tot_b, Eb[:, :, 0, 0:128], ALU.subtract)
                    v_.tensor_tensor(K[:, :, 0, :], tot_f, Ef[:, :, 0, 1:129], ALU.subtract)
                    v_.tensor_copy(K[:, :, 1, :], Eb[:, :, 1, 0:128]).then_inc(sem("lev_diff"), 1)
                    return
                B = LEVELS[n - 1]
                H = B // 2
                q, k = (qk[n % 2][:, i, :].rearrange("p (r b s) -> p r b s", r=8, s=B) for i in range(2))

                def rows(x, off):
                    return x.rearrange("p h t s -> p (h t) s")[:, :, off:off + P].rearrange("p r (b s) -> p r b s", s=B)

                f0, f1, b0 = rows(Ef, 0), rows(Ef, 1), rows(Eb, 0)
                nb_ = P // B
                mf = f0[:, :, :, H:H + 1].broadcast_to([P, 8, nb_, H])
                mb = b0[:, :, :, H:H + 1].broadcast_to([P, 8, nb_, H])
                v_.tensor_tensor(q[:, :, :, H:B], f1[:, :, :, H:B], mf, ALU.subtract)
                v_.tensor_tensor(k[:, :, :, 0:H], mf, f1[:, :, :, 0:H], ALU.subtract)
                v_.tensor_tensor(q[:, :, :, 0:H], mb, b0[:, :, :, 0:H], ALU.subtract)
                v_.tensor_tensor(k[:, :, :, H:B], b0[:, :, :, H:B], mb, ALU.subtract).then_inc(sem("lev_diff"), 1)

            def scaled(n):
                dve.wait_ge(sem("lev_exp"), n + 1)
                if n == 0:
                    Q, K = qk_of(n)
                    v_.tensor_tensor(Q, Q, qh, ALU.mult)
                    v_.tensor_tensor(K[:, :, 0, :], K[:, :, 0, :], kf[:, :, 0, :], ALU.mult)
                    v_.tensor_tensor(K[:, :, 1, :], K[:, :, 1, :], kb[:, :, 1, :], ALU.mult).then_inc(sem("lev_qk"), 1)
                    return
                B = LEVELS[n - 1]
                H = B // 2
                q, k = (qk[n % 2][:, i, :].rearrange("p (r b s) -> p r b s", r=8, s=B) for i in range(2))
                qf = qk[n % 2][:, 0, :]
                v_.tensor_tensor(qf, qf, hqT.rearrange("p h s -> p (h s)"), ALU.mult)
                kfv, kbv = (x.rearrange("p h s -> p (h s)").rearrange("p (r b s) -> p r b s", r=8, s=B)
                            for x in (kin[:, 0:4], kin[:, 4:8]))
                v_.tensor_tensor(k[:, :, :, 0:H], k[:, :, :, 0:H], kfv[:, :, :, 0:H], ALU.mult)
                v_.tensor_tensor(k[:, :, :, H:B], k[:, :, :, H:B], kbv[:, :, :, H:B], ALU.mult).then_inc(sem("lev_qk"), 1)

            def place(n):
                dve.wait_ge(sem("lev_mm"), n + 1)
                for t in range(TT):
                    src = psA[:, 2 * (n % 2) + t, :].rearrange("p (h s) -> p h s", h=4)
                    if n == 0:
                        dst = AT[:, t, :, P * (1 - t):P * (1 - t) + P]
                    else:
                        dst = AT[:, t, :, P * t:P * t + P]
                    if n <= 1:
                        ins = v_.tensor_copy(dst, src)
                    else:
                        if n <= 7:
                            m = cst("levels")[:, (n - 2) * P:(n - 1) * P]
                        else:
                            m = ident
                        m = m.bitcast(I32).unsqueeze(1).broadcast_to([P, 4, P])
                        ins = v_.copy_predicated(dst, m, src)
                ins.then_inc(sem("lev_placed"), 1)
                dve.wait_ge(sem("lev_placed"), n + 1)

            nlev = len(LEVELS) + 2

            def level(n):
                if n + 1 < nlev - 1:
                    diffs(n + 1)
                if n < nlev - 1:
                    scaled(n)
                else:
                    dve.wait_ge(sem("lev_mm"), n - 1)
                    v_.tensor_tensor(qk[n % 2][:, 1, :], kin[:, 0:4].rearrange("p h s -> p (h s)"),
                                     kin[:, 4:8].rearrange("p h s -> p (h s)"), ALU.add).then_inc(sem("lev_qk"), 1)
                if n >= 1:
                    place(n - 1)

            for j, (what, c0) in enumerate(IN1_COLS):
                lo(IN1 + j + 2)
                half = (j % 2) * 2
                two = psW[:, j % 3, :].rearrange("p (a s) -> p a s", a=2)
                if j < 4:
                    angles(j)
                if what == "g":
                    dve.wait_ge(sem("gsig_ready"), j % 2 + 1)
                    v_.tensor_tensor(gT[:, half:half + 2, :], gT[:, half:half + 2, :], two, ALU.mult).then_inc(sem("in1_read_dve"), 1)
                elif what == "hq":
                    dve.wait_ge(sem("wt_used"), IN1 + j + 1)
                    v_.tensor_copy(hqT[:, half:half + 2, :], two).then_inc(sem("in1_read_dve"), 1)
                if j == 4:
                    for i in range(2):
                        v_.tensor_tensor_reduce(lamp[:, i, :], lamr[:, 2 * i, :], lamr[:, 2 * i + 1, :], 1.0, 0.0,
                                                ALU.mult, ALU.add, lamt[:, i:i + 1]).then_inc(sem("lam_ready"), 1)
                if j == 5:
                    dve.wait_ge(sem("in1_read_act"), 4)
                    dve.wait_ge(sem("lb_ready"), 1)
                    for d in range(8):
                        v_.tensor_scalar(kin[:, d, :], kin[:, d, :], omlb[:, d:d + 1], None, ALU.mult)
                if j in (7, 8):
                    if j == 7:
                        dve.wait_ge(sem("act_set"), 3)
                        dve.wait_ge(sem("lam_ready"), 2)
                        v_.memset(E[:, :, :, 0:1], 0.0)
                    for d in range(4 * (j - 7), 4 * (j - 7) + 4):
                        dve.wait_ge(sem("lf_ready"), d + 1)
                        for t in range(TT):
                            ins = v_.tensor_tensor_scan(E[:, d, t, 1:129], ones[:, :], lf[:, d, P * t:P * t + P], 0.0,
                                                        ALU.mult, ALU.add)
                if j == 8:
                    link(ins)
                    dve.wait_ge(sem("lam_exp"), 1)
                    v_.scalar_tensor_tensor(nlam, lamt[:, 3:4], -LAMBDA_INIT, lamt[:, 2:3], ALU.add,
                                            ALU.subtract).then_inc(sem("setup_done"), 1)
                if j == 9:
                    diffs(0)
                if j in LEVEL_AT:
                    level(LEVEL_AT.index(j))

            def rotary(dst, src, rot, table, width, tmp):
                c = trig[:, table, 0, :]
                s = trig[:, table, 1, :]
                if width == 2:
                    c, s = (x.unsqueeze(1).broadcast_to([P, 2, S]) for x in (c, s))
                link(v_.tensor_tensor(tmp, rot, s, ALU.mult))
                link(v_.tensor_tensor(dst, src, c, ALU.mult))
                return v_.tensor_tensor(dst, dst, tmp, ALU.add)

            def rotate(n):
                x = (qT, kT)[n % 2][:, 2 * (n // 2):2 * (n // 2) + 2, :]
                dve.wait_ge(sem("rot1"), n + 1)
                if n:
                    dve.wait_ge(sem("rot1_done"), n)
                rotary(x, x, psX[:, n, :].rearrange("p (a s) -> p a s", a=2), 0, 2,
                       rot1.rearrange("p (a s) -> p a s", a=2)).then_inc(sem("rot1_done"), 1)

            for n in range(len(LEVEL_AT), nlev):
                level(n)
                if n >= nlev - 3:
                    rotate(n - nlev + 3)
            rotate(3)
            place(nlev - 1)

            def head_norm(tag, src, gain, step, silu):
                for half in range(2):
                    hs = slice(2 * half, 2 * half + 2)
                    dve.wait_ge(sem(f"{tag}_root"), half + 1)
                    link(v_.reciprocal(hn_rt[:, hs, :], hn_rt[:, hs, :]))
                    ins = v_.scalar_tensor_tensor(hn_of[:, hs, :], src(half), gain, hn_rt[:, hs, :], ALU.mult, ALU.mult)
                    if silu:
                        link(ins)
                        ins = v_.tensor_tensor(hn_of[:, hs, :], hn_of[:, hs, :], gT[:, hs, :], ALU.mult)
                    ins.then_inc(sem(f"{tag}_of"), 1)
                for half in range(2):
                    dve.wait_ge(sem(f"{tag}_ohi"), half + 1)
                    at = step + 2 * half
                    v_.tensor_tensor(ol[:, at:at + 2, :], hn_of[:, 2 * half:2 * half + 2, :], oh[:, at:at + 2, :].bitcast(F32),
                                     ALU.subtract).then_inc(sem(f"{tag}_olo"), 1)

            head_norm("hg", lambda h: psA[:, 2 + h, :].rearrange("p (a s) -> p a s", a=2), colA("hgnorm"), 4, True)

            lo(OUT1 + 2)
            dve.wait_ge(sem("hg_olo"), 2)

            for n in range(8):
                dve.wait_ge(sem("da_sc"), n + 1)
                sc = psX[:, 2 * (n % 2):2 * (n % 2) + 2, 0:256]
                link(v_.tensor_reduce(da_s[:, 2 * n:2 * n + 2], sc, AXX, ALU.max))
                v_.tensor_scalar(da_s[:, 16 + 2 * n:18 + 2 * n], da_s[:, 2 * n:2 * n + 2], -0.125, None,
                                 ALU.mult).then_inc(sem("da_max"), 1)
                dve.wait_ge(sem("da_exp"), 2 * n + 2)
                link(v_.reciprocal(da_s[:, 48 + 2 * n:50 + 2 * n], da_s[:, 32 + 2 * n:34 + 2 * n]))
                if n >= 2:
                    dve.wait_ge(sem("da_pt"), n - 1)
                v_.tensor_scalar(da_d[n % 2][:, 0, :], ident, da_s[:, 48 + 2 * n:49 + 2 * n], None, ALU.mult)
                v_.tensor_scalar(da_d[n % 2][:, 1, :], ident, da_s[:, 49 + 2 * n:50 + 2 * n], nlam, ALU.mult,
                                 ALU.mult).then_inc(sem("da_diag"), 1)
            head_norm("da", lambda h: psA[:, 2 + h, :].rearrange("p (a s) -> p a s", a=2), subg, 0, False)

            for j in range(4):
                if j:
                    lo(OUT1 + j + 2)
                dve.wait_ge(sem("wt_used"), OUT1 + j + 1)
                x = xT[:, 2 * j:2 * j + 2, :]
                v_.tensor_tensor(x, x, psW[:, j % 3, :].rearrange("p (a s) -> p a s", a=2), ALU.add).then_inc(sem("x_ready"), 1)

            gatep = psW[:, 0, :].rearrange("p (a s) -> p a s", a=2)
            upp = psW[:, 1, :].rearrange("p (a s) -> p a s", a=2)

            def conv(f, nb_, i, first):
                dve.wait_ge(sem("wt_used"), nb_ + 1 + 3 * i)
                if first:
                    dve.wait_ge(sem("ge_ready"), FSTEP * f + i + first)
                for t in range(2):
                    def tap(j):
                        if isinstance(i, int):
                            return colsA[:, 22 * j + 2 * (i + first) + t:22 * j + 2 * (i + first) + t + 1]
                        return colsA[:, bass.ds(2 * i + (22 * j + 2 * first + t), 1)]
                    ft = f_t[:, t, :]
                    link(v_.tensor_scalar(ft, gatep[:, t, :], tap(1), tap(3), ALU.mult, ALU.add))
                    link(v_.scalar_tensor_tensor(ft[:, 1:S], gatep[:, t, 0:S - 1], tap(0), ft[:, 1:S], ALU.mult, ALU.add))
                    ins = v_.scalar_tensor_tensor(ft[:, 0:S - 1], gatep[:, t, 1:S], tap(2), ft[:, 0:S - 1], ALU.mult, ALU.add)
                ins.then_inc(sem("conv_ready"), 1)

            def ada_piece(u, r=0, ks=KT, group=None):
                dve.wait_ge(sem(f"ada{r}_loaded"), 16 * (group if r else u) + 16)
                if r:
                    dve.wait_ge(sem("ada0_used"), u + 1)
                elif isinstance(u, int) and u == 0:
                    dve.wait_ge(sem("cond_ready"), 1)
                else:
                    dve.wait_ge(sem("ada_sum"), u)
                w, acc = kview(adar[r], ks), adacc[:, 0:2048 // ks]
                for k in range(ks):
                    c = condT[:, 4 * r + k:4 * r + k + 1]
                    if r == 0 and k == 0:
                        ins = v_.tensor_scalar(acc, w[:, k, :], c, None, ALU.mult)
                    else:
                        ins = v_.scalar_tensor_tensor(acc, w[:, k, :], c, acc, ALU.mult, ALU.add)
                    if k < ks - 1:
                        link(ins)
                ins.then_inc(sem(f"ada{r}_used"), 1)

            def hidden(f, nb_, i, first):
                dve.wait_ge(sem("wt_used"), nb_ + 1 + 3 * i)
                dve.wait_ge(sem("ge_ready"), FSTEP * f + 1 + i + first)
                if f > 0 or first:
                    dve.wait_ge(sem("flo_ready"), FSTEP * f + i + first)
                v_.tensor_tensor(f_a, f_g, upp, ALU.mult).then_inc(sem("actf_ready"), 1)

            def hidden_lo(f, i, first, q=0):
                dve.wait_ge(sem("fhi_ready"), FSTEP * f + 1 + i + first)
                dve.wait_ge(sem("actf_ready"), FSTEP * f + 1 + i + first)
                v_.tensor_tensor(ol[:, q:q + 2, :], f_a, oh[:, q:q + 2, :].bitcast(F32), ALU.subtract).then_inc(sem("flo_ready"), 1)

            def piece(f, i, part):
                if f == 0 and part:
                    ada_piece(i + 1)
                if f == 1:
                    ada_piece(i + 1 + FSTEP, part, 4, i + 1)
                if f == 2 and part and isinstance(i, int) and i + 1 < ADA_TAIL:
                    ada_piece(i + 1 + 2 * FSTEP)

            def step(f, b, i):
                last = isinstance(i, int) and i == FSTEP - 2
                if f == 0:
                    conv(f, b + 2, i, 1)
                lo(b + 5, i)
                piece(f, i, 0)
                hidden(f, b + 3, i, 1)
                if last:
                    hidden_lo(f, i, 1, 2)
                    piece(f, i, 1)
                lo(b + 6, i)
                if not last:
                    piece(f, i, 1)
                lo(b + 7, i)
                if not last:
                    hidden_lo(f, i, 1)

            def ffn(b, f, gate):
                lo(b + 2)
                if f == 0:
                    conv(f, b, 0, 0)
                piece(f, -1, 0)
                lo(b + 3)
                hidden(f, b + 1, 0, 0)
                piece(f, -1, 1)
                lo(b + 4)
                hidden_lo(f, 0, 0)
                peel = ADA_TAIL - 1 if f == 2 else 0
                for i in range(peel):
                    step(f, b, i)
                links, start = [11, 6, 0][f], chain[0]
                chain[1] = links
                with dve.Fori(peel, FSTEP - 2) as i:
                    chain[2] = i
                    step(f, b, i)
                assert chain[0] - start == links, (chain[0] - start, links)
                chain[0], chain[1], chain[2] = start + links * (FSTEP - 2), 0, 0
                step(f, b, FSTEP - 2)
                if f:
                    modulation((f + 1) * FSTEP if f == 1 else 2 * FSTEP + ADA_TAIL, MOD_AT[f], MOD_AT[f + 1])
                    g = modT[:, 48 * f - 32:48 * f - 24]
                    link(v_.tensor_scalar(g, g, 0.5, None, ALU.mult))
                for k in range(KT):
                    if k % 2 == 0:
                        dve.wait_ge(sem("acc_done"), 3 * f + k // 2 + 1) if k < 6 else dve.wait_ge(sem("wt_used"), b + 33)
                    if gate is None:
                        ins = v_.tensor_tensor(xT[:, k, :], xT[:, k, :], accv[:, k, :], ALU.add)
                    else:
                        ins = v_.scalar_tensor_tensor(xT[:, k, :], accv[:, k, :], gate(k), xT[:, k, :], ALU.mult, ALU.add)
                    ins.then_inc(sem("x_ready"), 1)

            norm(1, lambda k: colA("norm_ffn", k), lambda k: zero)
            ffn(FFN1, 0, None)

            norm(2, lambda k: colA("norm_ple", k), lambda k: zero)
            lo(PLE + 2)
            for j in range(4):
                lo(PGATE + j + 2)
                dve.wait_ge(sem("pg_sig"), j + 1)
                dve.wait_ge(sem("wt_used"), PLE + 1)
                v = slice(2 * j, 2 * j + 2)
                sg = f_s[:, j % 2, :].rearrange("p (a s) -> p a s", a=2)
                link(v_.tensor_tensor(sg, sg, accv[:, v, :], ALU.mult))
                v_.tensor_tensor(xT[:, v, :], xT[:, v, :], sg, ALU.add).then_inc(sem("x_ready"), 1)
            norm(3, lambda k: f_s[:, 0, k:k + 1], lambda k: modT[:, k:k + 1])
            link(v_.reciprocal(rstd[:, :], rootv[:, :]))
            for k in range(KT):
                v_.scalar_tensor_tensor(xT[:, k, :], xT[:, k, :], colA("final", k), rstd[:, :],
                                        ALU.mult, ALU.mult).then_inc(sem("x_ready"), 1)
            ffn(FFN2, 1, lambda k: modT[:, 16 + k:17 + k])
            gains(1)
            gains(2)
            norm(4, lambda k: gain2[:, 8 + k:9 + k], lambda k: modT[:, 24 + k:25 + k])

            def normed(n):
                what = IN2_COLS[NORM_AT[n]][0]
                w = 256 if what == "misc" else 512
                dve.wait_ge(sem("m_root"), n + 1)
                link(v_.reciprocal(m_rt[:, 0:w], m_rt[:, 0:w]))
                gain = {"fq": foxg_q, "fk": colB("foxg", 1), "dq": dsag_q, "misc": colB("dsag", 1)}[what]
                dst = {"fq": fqT, "fk": fkT, "dq": dqT}.get(what)
                dst = dkT if dst is None else dst[:, 2 * (n % 2):2 * (n % 2) + 2, :].rearrange("p a s -> p (a s)")
                v_.scalar_tensor_tensor(dst, psW[:, NORM_AT[n] % 3, 0:w], gain, m_rt[:, 0:w], ALU.mult, ALU.mult).then_inc(sem("in2_read_dve"), 1)

            for j, (what, c0) in enumerate(IN2_COLS[:GB]):
                lo(IN2 + j + 2)
                if j - 1 in NORM_AT:
                    normed(NORM_AT.index(j - 1))
                if (what, c0) == ("misc", 1):
                    dve.wait_ge(sem("wt_used"), IN2 + j + 1)
                    v_.tensor_scalar(lgs[0][0:8, :], psA[0:8, 0, 0:S], ffb, None, ALU.add).then_inc(sem("ff_x"), 1)
            dve.wait_ge(sem("ff_x"), 1)
            link(v_.tensor_scalar(lgs[2][0:8, :], lgs[0][0:8, :], 0.0, None, ALU.min))
            dve.wait_ge(sem("ff_act"), 3)
            link(v_.tensor_tensor(lgs[2][0:8, :], lgs[2][0:8, :], lgs[1][0:8, :], ALU.subtract))
            link(v_.memset(Fc, 0.0))
            link(v_.tensor_tensor_scan(Fc[0:8, :], one[0:8, :].broadcast_to([8, S]), lgs[2][0:8, :], 0.0, ALU.mult, ALU.add))
            v_.tensor_copy(Fc[64:72, :], Fc[0:8, :]).then_inc(sem("F_ready"), 1)

            def rotate_pairs(n):
                if n >= 5:
                    return
                x, table = ((dqT[:, 0:2, :], 1), (dqT[:, 2:4, :], 1), (iqT, 2), (dkT, 1), (ikT, 2))[n]
                dve.wait_ge(sem("rot2"), n + 1)
                if n:
                    dve.wait_ge(sem("rot2_done"), n)
                two = n < 3
                r = psS[:, 0:512].rearrange("p (a s) -> p a s", a=2) if two else psS[:, 0:S]
                rotary(x, x, r, table, 2 if two else 1,
                       m_xn.rearrange("p (a s) -> p a s", a=2) if two else m_xn[:, 0:S]).then_inc(sem("rot2_done"), 1)

            def softmax_heads(tag, bias0, bias1, between=None):
                for h in range(8):
                    dve.wait_ge(sem(f"{tag}_sc"), h + 1)
                    if h >= 2:
                        dve.wait_ge(sem(f"{tag}_pt"), h - 1)
                    bank = psW[:, h % 3, :]
                    for qt in range(2):
                        c = 2 * h + qt
                        v, s, b = (m_p[h % 2][:, 0:128], bank[:, 0:128], bias0) if qt == 0 else (
                            m_p[h % 2][:, 128:384], bank[:, 128:384], bias1)
                        link(v_.tensor_tensor_reduce(v, s, b, 1.0, -3e38, ALU.add, ALU.max, m_s[:, c:c + 1]))
                        v_.tensor_scalar(m_s[:, 32 + c:33 + c], m_s[:, c:c + 1], -1.0, None, ALU.mult).then_inc(sem(f"{tag}_max"), 1)
                    dve.wait_ge(sem(f"{tag}_exp"), 2 * h + 2)
                    link(v_.reciprocal(m_s[:, 96 + 2 * h:98 + 2 * h], m_s[:, 64 + 2 * h:66 + 2 * h]))
                    for qt in range(2):
                        ins = v_.tensor_scalar(m_d[h % 2][:, qt, :], ident, m_s[:, 96 + 2 * h + qt:97 + 2 * h + qt], None, ALU.mult)
                    ins.then_inc(sem(f"{tag}_diag"), 1)
                    if between and h:
                        between(h - 1)

            def out_lo(tag, base):
                for c in range(2):
                    dve.wait_ge(sem(f"{tag}_ohi"), c + 1)
                    dst = slice(4 * base + 2 * c, 4 * base + 2 * c + 2)
                    v_.tensor_tensor(ol[:, dst, :], psA[:, 2 + c, :].rearrange("p (a s) -> p a s", a=2),
                                     oh[:, dst, :].bitcast(F32), ALU.subtract).then_inc(sem(f"{tag}_olo"), 1)

            causal = cst("causal")
            softmax_heads("fox", causal[:, P:2 * P], causal, rotate_pairs)
            out_lo("fox", 0)

            dve.wait_ge(sem("misc_act"), 3)
            link(v_.tensor_scalar(iwt, iwt, 8 ** -0.5, None, ALU.mult))
            for qt in range(2):
                w = P * (qt + 1)
                sc = (sc0, sc1)[qt]
                dve.wait_ge(sem("ix_relu"), qt + 1)
                for h in range(8):
                    r = reluv[:, (h % 4) * 2 * w + (h // 4) * w:(h % 4) * 2 * w + (h // 4) * w + w]
                    if h == 0:
                        ins = v_.tensor_scalar(sc, r, iwt[:, qt, 0:1], None, ALU.mult)
                    else:
                        ins = v_.scalar_tensor_tensor(sc, r, iwt[:, qt, h:h + 1], sc, ALU.mult, ALU.add)
                    if h < 7:
                        link(ins)
                ins.then_inc(sem("ix_sum"), 1)
                dve.wait_ge(sem("ix_sum"), qt + 1)
                d = sc[:, w - P:w]
                link(v_.tensor_tensor(d, d, cst("admit")[:, P:2 * P], ALU.add))
                for _r in range(TOPK // 8):
                    link(v_.max(top8, sc))
                    link(v_.match_replace(sc, top8, sc, PICKED))
                ins = v_.tensor_scalar(sc, sc, 0.5 * PICKED, BIG, ALU.is_gt, ALU.mult)
                link(ins)
                lo(IN2 + GB + 2 + qt)
            lo(BRANCH)
            lo(BRANCH + 1)
            softmax_heads("dsa", sc0, sc1)
            out_lo("dsa", 1)

            for c in range(2):
                lo(BRANCH + 2 * c + 2)
                lo(BRANCH + 2 * c + 3)
                dve.wait_ge(sem("wt_used"), BRANCH + 2 * c + 2)
                for t in range(2):
                    k = 4 * c + 2 * t
                    if t == 0:
                        dve.wait_ge(sem("gb_ready"), c + 1)
                    ya, yb = ((psX if c else psA)[:, i + t, :].rearrange("p (a s) -> p a s", a=2) for i in (0, 2))
                    ga, gb = gaS[:, k:k + 2, :], gbS[:, k:k + 2, :]
                    v_.tensor_tensor(ga, ga, ya, ALU.mult)
                    link(v_.tensor_tensor(gb, gb, yb, ALU.mult))
                    if c or t:
                        dve.wait_ge(sem("mg_hi"), 2 * c + t)
                        dve.wait_ge(sem("mg_lo"), 2 * c + t)
                    v_.tensor_tensor(mg, ga, gb, ALU.add).then_inc(sem("mg_ready"), 1)
                    dve.wait_ge(sem("mg_hi"), 2 * c + t + 1)
                    dve.wait_ge(sem("mg_ready"), 2 * c + t + 1)
                    v_.tensor_tensor(hl[:, k:k + 2, :], mg, hh[:, k:k + 2, :].bitcast(F32),
                                     ALU.subtract).then_inc(sem("mg_lo"), 1)
            for j in range(4):
                lo(OUT2 + j + 2)
                dve.wait_ge(sem("wt_used"), OUT2 + j + 1)
                for t in range(2):
                    k = 2 * j + t
                    v_.scalar_tensor_tensor(xT[:, k, :], psA[:, j, 256 * t:256 * t + 256], modT[:, 40 + k:41 + k],
                                            xT[:, k, :], ALU.mult, ALU.add).then_inc(sem("x_ready"), 1)
            norm(5, lambda k: gain2[:, 16 + k:17 + k], lambda k: modT[:, 48 + k:49 + k])
            ffn(FFN3, 2, lambda k: modT[:, 64 + k:65 + k])

        @block.tensor
        def _(pe):
            def have(b, i=0):
                pe.wait_ge(sem("lo_ready"), b + 1 + 3 * i)

            def mm3(dst, ws, w, xh, xl, start, stop):
                wh, wl = (w(kview(b, ws[1])) for b in (whi[ws[0] % 3], wlo[ws[0] % 3]))
                pe.matmul(dst, wh, xh, start=start, stop=False, skip_group_check=True)
                pe.matmul(dst, wh, xl, start=False, stop=False, skip_group_check=True)
                return pe.matmul(dst, wl, xh, start=False, stop=stop, skip_group_check=True)

            def mm3t(dst, ws, w, xh, xl, start, stop):
                wh, wl = (w(kview(b, ws[1])) for b in (whi[ws[0] % 3], wlo[ws[0] % 3]))
                pe.matmul(dst, xh, wh, start=start, stop=False, skip_group_check=True)
                pe.matmul(dst, xh, wl, start=False, stop=False, skip_group_check=True)
                return pe.matmul(dst, xl, wh, start=False, stop=stop, skip_group_check=True)

            def gemm(b, bank, xh, xl, i=0, first=None, merged=False):
                have(b, i)
                order = [(t, k) for t in range(2) for k in range(KT)]
                if first is not None or merged:
                    order = [(t, k) for k in range(KT) for t in range(2)]
                for t, k in order:
                    if first is not None and t == 0:
                        pe.wait_ge(sem("hlo_ready"), KT * first + k + 1)
                    if merged and t == 0 and k % 2 == 0:
                        pe.wait_ge(sem("mg_lo"), k // 2 + 1)
                    start = k == 0 and (t == 0 or not (merged or first is not None))
                    ins = mm3(bank[:, 256 * t:256 * t + 256], (b, KT), lambda w: w[:, k, P * t:P * t + P],
                              xh[:, k, :], xl[:, k, :], start, k == KT - 1)
                ins.then_inc(sem("wt_used"), 1)

            def gemm_tok(b, bank):
                have(b)
                for t in range(2):
                    for k in range(KT):
                        ins = mm3t(bank[:, 256 * t:256 * t + 256], (b, KT), lambda w: w[:, k, :],
                                   hh[:, k, P * t:P * t + P], hl[:, k, P * t:P * t + P], k == 0, k == KT - 1)
                ins.then_inc(sem("wt_used"), 1)

            def mean(m, k):
                pe.wait_ge(sem("sq_ready"), KT * m + k + 1)
                ins = pe.matmul(psS[:, 0:S], ones1k[:, :], nb[:, k, :], start=(k == 0), stop=(k == KT - 1),
                                skip_group_check=True)
                if k == KT - 1:
                    ins.then_inc(sem("mean_ready"), 1)

            def means(m):
                for k in range(KT):
                    mean(m, k)

            pe.wait_ge(sem("con_loaded"), 16)
            pe.wait_ge(sem("x_loaded"), 16)
            for k in range(KT):
                for t in range(TT):
                    ins = pe.transpose(accv[:, k, P * t:P * t + P], xtok[:, t, P * k:P * k + P], ident)
            ins.then_inc(sem("x_tr"), 1)
            pe.wait_ge(sem("small_loaded"), 16 * 16)
            pe.transpose(psS[:, 0:NROW_A], rowsA[0:NROW_A, :], ident[0:NROW_A, 0:NROW_A])
            pe.transpose(psS[:, P:P + NROW_B], rowsB[0:NROW_B, :], ident[0:NROW_B, 0:NROW_B]).then_inc(sem("cols_tr"), 1)
            pe.wait_ge(sem("cols_ready"), 1)
            pe.wait_ge(sem("small_set"), 1)
            means(0)
            pe.wait_ge(sem("p_loaded"), 16)
            for k in range(2):
                for t in range(TT):
                    ins = pe.transpose(psW[:, 2, 256 * k + P * t:256 * k + P * t + P], ptok[:, t, P * k:P * k + P], ident)
            ins.then_inc(sem("p_tr"), 1)

            nlev = len(LEVELS) + 2

            def level(n):
                pe.wait_ge(sem("lev_qk"), n + 1)
                if n >= 2:
                    pe.wait_ge(sem("lev_placed"), n - 1)
                for t in range(TT):
                    for h in range(4):
                        k = qk[n % 2][:, 1, :].rearrange("p (h s) -> p h s", h=4)[:, h, P * t:P * t + P]
                        tq = 1 - t if n == 0 else t
                        q = (hqT if n == nlev - 1 else qk[n % 2][:, 0, :].rearrange("p (h s) -> p h s", h=4))[:, h, P * tq:P * tq + P]
                        ins = pe.matmul(psA[:, 2 * (n % 2) + t, P * h:P * h + P], k, q, start=True, stop=True,
                                        skip_group_check=True)
                ins.then_inc(sem("lev_mm"), 1)

            for j, (what, c0) in enumerate(IN1_COLS):
                if j == 2:
                    pe.wait_ge(sem("p_lo"), 1)
                if j >= 3:
                    r = j - 3
                    if r < 4:
                        pe.wait_ge(sem("in1_read_act"), r + 1)
                    elif r < 8:
                        pe.wait_ge(sem("in1_read_dve"), r - 3)
                    else:
                        pe.wait_ge(sem("in1_read_act"), r - 3)
                if what in ("hv", "dv"):
                    gemm_tok(IN1 + j, psW[:, j % 3, :])
                else:
                    gemm(IN1 + j, psW[:, j % 3, :], hh, hl, first=0 if j == 0 else None)
                if j - 1 in LEVEL_AT:
                    level(LEVEL_AT.index(j - 1))

            for n in range(len([j for j in LEVEL_AT if j < 15]), nlev):
                level(n)
                if n >= nlev - 4:
                    m = n - nlev + 4
                    pe.wait_ge(sem("in1_read_act"), 12)
                    x = (qT, kT)[m % 2][:, 2 * (m // 2):2 * (m // 2) + 2, :].rearrange("p a s -> p (a s)")
                    pe.matmul(psX[:, m, :], rotA, x, start=True, stop=True).then_inc(sem("rot1"), 1)
            pe.wait_ge(sem("lev_placed"), nlev)
            pe.wait_ge(sem("in1_read_act"), 12)
            for h in range(4):
                for t in range(TT):
                    ins = pe.matmul(psA[:, 2 + h // 2, 256 * (h % 2):256 * (h % 2) + 256], hvt[:, t, P * h:P * h + P],
                                    AT[:, t, h, :], start=(t == 0 and h % 2 == 0), stop=(t == 1), skip_group_check=True)
                if h % 2:
                    ins.then_inc(sem("hg_o"), 1)
            def head_means(tag):
                for half in range(2):
                    pe.wait_ge(sem(f"{tag}_sq"), half + 1)
                    pe.matmul(psA[:, half, :], ones128[:, :], hn_sq[:, 2 * half:2 * half + 2, :].rearrange("p a s -> p (a s)"),
                              start=True, stop=True).then_inc(sem(f"{tag}_mean"), 1)

            head_means("hg")
            pe.wait_ge(sem("rot1_done"), 4)
            pe.wait_ge(sem("hg_of"), 2)

            def scores(n):
                h, qt = n // 2, n % 2
                if n >= 2:
                    pe.wait_ge(sem("da_exp"), 2 * (n - 2) + 2)
                for m in range(2):
                    r = slice(64 * m, 64 * m + 64)
                    ins = pe.matmul(psX[:, 2 * (n % 2) + m, 0:256], qT[r, h, P * qt:P * qt + P], kT[r, h, :],
                                    start=True, stop=True, skip_group_check=True)
                ins.then_inc(sem("da_sc"), 1)

            def da_pt(n):
                pe.wait_ge(sem("da_diag"), n + 1)
                if n >= 2:
                    pe.wait_ge(sem("da_wt"), n - 1)
                for kt in range(2):
                    for m in range(2):
                        ins = pe.matmul(psA[:, n % 2, P * kt:P * kt + P], da_p[n % 2][:, m, P * kt:P * kt + P],
                                        da_d[n % 2][:, m, :], start=(kt == 0 and m == 0), stop=(m == 1), skip_group_check=True)
                ins.then_inc(sem("da_pt"), 1)

            def da_pv(h):
                pe.wait_ge(sem("da_wt"), 2 * h + 2)
                for kt in range(2):
                    ins = pe.matmul(psA[:, 2 + h // 2, 256 * (h % 2):256 * (h % 2) + 256], dvt[:, kt, P * h:P * h + P],
                                    da_w[h % 2][:, kt, :], start=(kt == 0 and h % 2 == 0), stop=(kt == 1), skip_group_check=True)
                ins.then_inc(sem("da_oh"), 1)

            scores(0)
            for n in range(8):
                if n < 7:
                    scores(n + 1)
                da_pt(n)
                if n >= 2 and n % 2 == 0:
                    da_pv(n // 2 - 1)
            da_pv(3)
            head_means("da")

            def out_half(j, ks, t0_start, stop):
                have(OUT1 + j)
                for t in range(2):
                    for k in ks:
                        ins = mm3(psW[:, j % 3, 256 * t:256 * t + 256], (OUT1 + j, KT), lambda w: w[:, k, P * t:P * t + P],
                                  oh[:, k, :], ol[:, k, :], t0_start and t == 0 and k == ks[0], stop and k == ks[-1])
                return ins

            pe.wait_ge(sem("hg_olo"), 2)
            pe.wait_ge(sem("da_exp"), 16)
            for j in range(3):
                out_half(j, range(4, KT), True, False)
            pe.wait_ge(sem("da_olo"), 2)
            for j in range(3):
                out_half(j, range(4), False, True).then_inc(sem("wt_used"), 1)
            pe.wait_ge(sem("x_ready"), X_OUT1 + 1)
            gemm(OUT1 + 3, psW[:, 0, :], oh, ol)

            def down(b, i, f, first):
                have(b, i)
                pe.wait_ge(sem("flo_ready"), FSTEP * f + i + first)
                for o in range(KT):
                    for k in range(2):
                        ins = mm3(accv[:, o, :], (b, 2), lambda w: w[:, k, P * o:P * o + P], oh[:, k, :], ol[:, k, :], False, False)
                ins.then_inc(sem("wt_used"), 1)

            def ada_sums(f, i):
                if f == 1:
                    pe.wait_ge(sem("ada1_used"), i + 1)
                else:
                    pe.wait_ge(sem("ada0_used"), f * FSTEP + i + 1)
                n = 4 if f == 1 else 2
                c0 = 256 + n * i + MOD_AT[f]
                for k in range(n):
                    dst = psS[:, c0 + k:c0 + k + 1] if isinstance(i, int) else psS[:, bass.ds(c0 + k, 1)]
                    ins = pe.matmul(dst, adacc[:, P * k:P * k + P], ones[:, 0:1], start=True, stop=True,
                                    skip_group_check=True)
                ins.then_inc(sem("ada_sum"), 1)

            def ffn(b, f, m, acc_free):
                pe.wait_ge(sem(acc_free[0]), acc_free[1])
                for a in range(4):
                    pe.matmul(psA[:, a, :], zeros[:, :], zeros[:, 0:1].broadcast_to([P, 512]), start=True, stop=False, skip_group_check=True)
                gemm(b, psW[:, 0, :], hh, hl, first=m)
                gemm(b + 1, psW[:, 1, :], hh, hl)

                def step(i):
                    pe.wait_ge(sem("ge_ready" if f else "conv_ready"), FSTEP * f + i + 1)
                    gemm(b + 2, psW[:, 0, :], hh, hl, i)
                    if f == 1:
                        ada_sums(f, i)
                    pe.wait_ge(sem("actf_ready"), FSTEP * f + i + 1)
                    gemm(b + 3, psW[:, 1, :], hh, hl, i)
                    if f == 0 or (f == 2 and isinstance(i, int) and i < ADA_TAIL):
                        ada_sums(f, i)
                    down(b + 4, i, f, 1)

                peel = ADA_TAIL if f == 2 else 0
                for i in range(peel):
                    step(i)
                with pe.Fori(peel, FSTEP - 2) as i:
                    step(i)
                step(FSTEP - 2)
                have(b + 32)
                pe.wait_ge(sem("flo_ready"), FSTEP * (f + 1))
                for o in range(KT):
                    for k in range(2):
                        ins = mm3(accv[:, o, :], (b + 32, 2), lambda w: w[:, k, P * o:P * o + P], oh[:, 2 + k, :], ol[:, 2 + k, :],
                                  False, k == 1)
                    if o % 2:
                        ins.then_inc(sem("acc_done" if o < KT - 1 else "wt_used"), 1)
                    if o == 1 and f < 2:
                        ada_sums(f, FSTEP - 1)
                    if o in (3, 5, 7) and f < 2:
                        mean(2 * f + 2, o - 3)
                        mean(2 * f + 2, o - 2)
                if f < 2:
                    mean(2 * f + 2, 6)
                    mean(2 * f + 2, 7)

            means(1)
            ffn(FFN1, 0, 1, ("da_of", 2))

            pe.wait_ge(sem("x_ready"), X_FFN1 + KT)
            have(PLE)
            for o in range(KT):
                for k in range(2):
                    ins = mm3(accv[:, o, :], (PLE, 2), lambda w: w[:, k, P * o:P * o + P], pTh[:, k, :], pTl[:, k, :],
                              o % 2 == 0 and k == 0, k == 1)
            ins.then_inc(sem("wt_used"), 1)
            for j in range(4):
                if j == 3:
                    pe.wait_ge(sem("pg_sig"), 1)
                gemm(PGATE + j, psW[:, j % 3, :], hh, hl, first=2 if j == 0 else None)
            pe.wait_ge(sem("pg_sig"), 2)
            for k in range(KT):
                mean(3, k)
            for k in range(KT):
                pe.wait_ge(sem("sq2_ready"), k + 1)
                ins = pe.matmul(psW[:, 1, 0:S], ones1k[:, :], nb2[:, k, :], start=(k == 0), stop=(k == KT - 1))
            ins.then_inc(sem("mean2_ready"), 1)
            ffn(FFN2, 1, 3, ("x_ready", X_PGATE + 4))


            def head_mean(n):
                w = 256 if IN2_COLS[NORM_AT[n]][0] == "misc" else 512
                pe.wait_ge(sem("m_sq"), n + 1)
                if n:
                    pe.wait_ge(sem("m_root"), n)
                pe.matmul(psS[:, 0:w], mean64, m_sq[:, 0:w], start=True, stop=True).then_inc(sem("m_mean"), 1)

            plain = [j for j in range(GB) if j not in NORM_AT and j != NORM_AT[-1] + 1]
            for j, (what, c0) in enumerate(IN2_COLS[:GB]):
                b = IN2 + j
                bank = psW[:, j % 3, :]
                if j - 3 in NORM_AT:
                    pe.wait_ge(sem("in2_read_dve"), NORM_AT.index(j - 3) + 1)
                elif j - 3 in plain:
                    pe.wait_ge(sem("in2_read_act"), plain.index(j - 3) + 1)
                if what == "fv":
                    gemm_tok(b, bank)
                elif (what, c0) == ("misc", 1):
                    have(b)
                    for k in range(KT):
                        mm3(psA[:, 0, 0:S], (b, KT), lambda w: w[:, k, 8:136], hh[:, k, :], hl[:, k, :], k == 0, k == KT - 1)
                    for t in range(TT):
                        for k in range(KT):
                            mm3t(psA[:, 1, 8 * t:8 * t + 8], (b, KT), lambda w: w[:, k, 0:8],
                                 hh[:, k, P * t:P * t + P], hl[:, k, P * t:P * t + P], k == 0, k == KT - 1)
                        for k in range(KT):
                            ins = mm3t(psA[:, 1, P + 64 * t:P + 64 * t + 64], (b, KT), lambda w: w[:, k, 64:128],
                                       hh[:, k, P * t:P * t + P], hl[:, k, P * t:P * t + P], k == 0, k == KT - 1)
                    ins.then_inc(sem("wt_used"), 1)
                else:
                    gemm(b, bank, hh, hl, first=4 if j == 0 else None)
                if j - 1 in NORM_AT:
                    head_mean(NORM_AT.index(j - 1))
            pe.wait_ge(sem("in2_read_dve"), 7)
            pe.wait_ge(sem("misc_act"), 3)
            pe.wait_ge(sem("in2_read_act"), len(plain))
            pe.wait_ge(sem("ff_x"), 1)
            def rotate_pairs(n):
                if n >= 5:
                    return
                if n:
                    pe.wait_ge(sem("rot2_done"), n)
                rot, x = ((rotA, dqT[:, 0:2, :]), (rotA, dqT[:, 2:4, :]), (rotI, iqT), (rotA, dkT), (rotI, ikT))[n]
                if n < 3:
                    x = x.rearrange("p a s -> p (a s)")
                pe.matmul(psS[:, 0:512 if n < 3 else S], rot, x, start=True, stop=True).then_inc(sem("rot2"), 1)

            pe.wait_ge(sem("F_ready"), 1)

            def softmax_heads(tag, score, v_of, prev, between=None):
                def sc(h):
                    if h >= 3:
                        pe.wait_ge(sem(f"{tag}_max"), 2 * (h - 3) + 2)
                    score(h, psW[:, h % 3, :]).then_inc(sem(f"{tag}_sc"), 1)

                def pt(h):
                    pe.wait_ge(sem(f"{tag}_diag"), h + 1)
                    if h >= 2:
                        pe.wait_ge(sem(f"{tag}_wt"), h - 1)
                    p, d = m_p[h % 2], m_d[h % 2]
                    bank = psA[:, h % 2, :]
                    pe.matmul(bank[:, 0:128], p[:, 0:128], d[:, 0, :], start=True, stop=True, skip_group_check=True)
                    pe.matmul(bank[:, 128:256], p[:, 128:256], d[:, 1, :], start=False, stop=True, skip_group_check=True)
                    pe.matmul(bank[:, 256:384], p[:, 256:384], d[:, 1, :], start=False, stop=True, skip_group_check=True).then_inc(sem(f"{tag}_pt"), 1)

                def pv(h):
                    pe.wait_ge(sem(f"{tag}_wt"), h + 1)
                    w = m_w[h % 2]
                    rows = slice(64 * (h % 2), 64 * (h % 2) + 64)
                    t = h // 2
                    dst = psA[rows, 2 + t // 2, 256 * (t % 2):256 * (t % 2) + 256]
                    pe.matmul(dst, v_of(h, 0), w[:, 0:256], start=(t % 2 == 0), stop=False, skip_group_check=True)
                    pe.matmul(dst[:, P:2 * P], v_of(h, 1), w[:, 256:384], start=False, stop=True,
                              skip_group_check=True).then_inc(sem(f"{tag}_pv"), 1)

                if prev:
                    pe.wait_ge(sem(prev[0]), prev[1])
                sc(0)
                sc(1)
                pt(0)
                for h in range(8):
                    if h + 2 < 8:
                        sc(h + 2)
                    if between:
                        between(h)
                    if h + 1 < 8:
                        pt(h + 1)
                    pv(h)

            def fox_score(h, bank):
                r = slice(64 * (h % 2), 64 * (h % 2) + 64)
                for qt in range(2):
                    w = P * (qt + 1)
                    dst = bank[:, P * qt:P * qt + w]
                    q = slice(P * qt, P * qt + P)
                    pe.matmul(dst, fqT[r, h // 2, q], fkT[r, h // 2, 0:w], start=(qt == 0), stop=False, skip_group_check=True)
                    c = 64 * (h % 2) + h
                    pe.matmul(dst, Fc[r, q], ident[r, c:c + 1].broadcast_to([64, w]), start=False, stop=False, skip_group_check=True)
                    ins = pe.matmul(dst, negid[r, c:c + 1].broadcast_to([64, P]), Fc[r, 0:w], start=False, stop=True, skip_group_check=True)
                return ins

            pe.wait_ge(sem("setup_done"), 1)
            softmax_heads("fox", fox_score, lambda h, kt: fvt[:, kt, 64 * h:64 * h + 64], None, rotate_pairs)

            pe.wait_ge(sem("fox_wt"), 8)
            pe.wait_ge(sem("fox_olo"), 2)
            pe.wait_ge(sem("rot2_done"), 5)
            for qt in range(2):
                w = P * (qt + 1)
                if qt == 1:
                    pe.wait_ge(sem("ix_relu"), 1)
                for h in range(8):
                    t = h % 4
                    r = slice(32 * t, 32 * t + 32)
                    ins = pe.matmul(psA[:, t, (h // 4) * w:(h // 4) * w + w], iqT[r, h // 4, P * qt:P * qt + P], ikT[r, 0:w],
                                    start=(h < 4), stop=True, skip_group_check=True, tile_position=(32 * t, 0))
                ins.then_inc(sem("ix_dots"), 1)

            def dsa_score(h, bank):
                r = slice(64 * (h % 2), 64 * (h % 2) + 64)
                for qt in range(2):
                    w = P * (qt + 1)
                    ins = pe.matmul(bank[:, P * qt:P * qt + w], dqT[r, h // 2, P * qt:P * qt + P], dkT[r, 0:w],
                                    start=(qt == 0), stop=True, skip_group_check=True)
                return ins

            pe.wait_ge(sem("fox_max"), 16)
            for c in range(4):
                gemm(IN2 + GB + c, psX[:, c, :], hh, hl)
            pe.wait_ge(sem("ix_relu"), 2)
            softmax_heads("dsa", dsa_score, lambda h, kt: dvt2[:, kt, :], ("gb_read", 4))

            pe.wait_ge(sem("fox_olo"), 2)
            pe.wait_ge(sem("dsa_olo"), 2)
            for j in range(4):
                b, c, br = BRANCH + j, j // 2, j % 2
                have(b)
                for o in range(4):
                    for k in range(4):
                        ins = mm3((psX if c else psA)[:, 2 * br + o // 2, 256 * (o % 2):256 * (o % 2) + 256], (b, 4),
                                  lambda w: w[:, k, P * o:P * o + P], oh[:, 4 * br + k, :], ol[:, 4 * br + k, :],
                                  k == 0 and o % 2 == 0, k == 3)
                ins.then_inc(sem("wt_used"), 1)
            for j in range(4):
                gemm(OUT2 + j, psA[:, j, :], hh, hl, merged=j == 0)
            means(5)
            ffn(FFN3, 2, 5, ("x_ready", X_OUT2 + KT))
            pe.wait_ge(sem("x_ready"), X_END)
            for t in range(TT):
                for k in range(KT):
                    ins = pe.transpose(psA[:, 2 * t + k // 4, P * (k % 4):P * (k % 4) + P],
                                       xT[:, k, P * t:P * t + P], ident)
                ins.then_inc(sem("out_tr"), 1)


_NAMES = ["x", "p", "positions", "norm_mix_g", "w_in", "lam_q1", "lam_k1", "lam_q2", "lam_k2", "da_subln_g",
          "hg_lb_gamma", "hg_norm_g", "w_out", "norm_ffn_g", "w_ffn_gate", "w_ffn_up", "ffn_conv_w", "ffn_conv_b",
          "w_ffn_down", "norm_ple_g", "w_ple", "w_ple_gate", "final_norm_g", "c_2", "positions_2", "ada_w_2",
          "ada_b_2", "norm_g_2", "ffn1_w1_2", "ffn1_w3_2", "ffn1_w2_2", "w_in_2", "fox_f_bias_2", "fox_qk_g_2",
          "dsa_qk_g_2", "w_br_fox_2", "w_br_dsa_2", "w_out_2", "ffn2_w1_2", "ffn2_w3_2", "ffn2_w2_2"]


def kernel(**inputs):
    import concourse.bacc as bacc
    from concourse.bass_utils import run_bass_kernel_spmd

    nc = bacc.Bacc("TRN2", target_bir_lowering=False, num_devices=1)
    arrays, args = {}, {}
    for name in _NAMES:
        a = np.ascontiguousarray(inputs[name])
        arrays[f"in_{name}"] = a
        args[name] = nc.dram_tensor(f"in_{name}", a.shape, mybir.dt.from_np(a.dtype), kind="ExternalInput").ap()
    arrays["in_consts"] = constants()
    args["consts"] = nc.dram_tensor("in_consts", (P, CONST_N), F32, kind="ExternalInput").ap()
    out = nc.dram_tensor("out_x", (1, S, D), F32, kind="ExternalOutput").ap()
    two_blocks(nc, args, out)
    r = run_bass_kernel_spmd(nc, [arrays], core_ids=[0])
    return r.results[0]["out_x"]
```
